# Optimizing a Trainium2 kernel written in Bass

```python
import jax
import jax.numpy as jnp
from jax import lax

D_MODEL = 1024
BATCH = 1
SEQ = 256
DEPTH = 1

PLE_DIM = 256
EPS = 1e-6

GLA_HEADS = 4
GLA_DK = 128
GLA_DV = 256
GLA_QK_W = GLA_HEADS * GLA_DK
GLA_V_W = GLA_HEADS * GLA_DV
GLA_RANK = 16
GLA_TAU = 16.0
GLA_CHUNK = 64

ATT_GROUPS = ((128, 1), (512, 4), (2048, 16))
ATT_HEADS_PER_GROUP = 4
ATT_HEAD_DIM = 64
ATT_HEADS = ATT_HEADS_PER_GROUP * len(ATT_GROUPS)
ATT_W = ATT_HEADS * ATT_HEAD_DIM
ATT_OUT_W = ATT_HEADS_PER_GROUP * ATT_HEAD_DIM
ROT_DIM = ATT_HEAD_DIM // 4
ROPE_THETA = 500000.0

N_EXPERTS = 32
TOP_K = 4
D_EXPERT = D_MODEL
SWIGLU_ALPHA = 1.702
SWIGLU_LIMIT = 7.0

IN_SPLITS = (GLA_QK_W, GLA_QK_W, GLA_V_W, GLA_V_W, 2 * GLA_RANK, ATT_W, ATT_W, ATT_W, D_MODEL, D_MODEL)
IN_COLS = sum(IN_SPLITS)

kernel_name = 'hybrid_gla_dilated_moe_encoder'

def rmsnorm(x, g):
    xf = x.astype(jnp.float32)
    y = xf * lax.rsqrt(jnp.mean(xf * xf, axis=-1, keepdims=True) + EPS)
    return (y * g.astype(jnp.float32)).astype(x.dtype)

def partial_rotary(t, positions):
    half = ROT_DIM // 2
    inv_freq = ROPE_THETA ** (-jnp.arange(0, ROT_DIM, 2, dtype=jnp.float32) / ROT_DIM)
    ang = positions.astype(jnp.float32)[..., None] * inv_freq
    cos = jnp.cos(ang)[:, :, None, :]
    sin = jnp.sin(ang)[:, :, None, :]
    tr = t[..., :ROT_DIM].astype(jnp.float32)
    t1, t2 = tr[..., :half], tr[..., half:]
    rot = jnp.concatenate([t1 * cos - t2 * sin, t2 * cos + t1 * sin], axis=-1)
    return jnp.concatenate([rot.astype(t.dtype), t[..., ROT_DIM:]], axis=-1)

def gla_chunked(q, k, v, g, strict):
    B, S, H, DK = q.shape
    DV = v.shape[-1]
    C = GLA_CHUNK
    N = S // C
    f32 = jnp.float32
    q = q.astype(f32).reshape(B, N, C, H, DK) * (DK ** -0.5)
    k = k.astype(f32).reshape(B, N, C, H, DK)
    v = v.astype(f32).reshape(B, N, C, H, DV)
    b = jnp.cumsum(g.astype(f32).reshape(B, N, C, H, DK), axis=2)
    b_ref = b[:, :, C // 2 - 1:C // 2]
    b_last = b[:, :, C - 1:C]
    scores = jnp.einsum('bnihd,bnjhd->bnhij', q * jnp.exp(b - b_ref), k * jnp.exp(b_ref - b))
    mask = jnp.tril(jnp.ones((C, C), dtype=bool), -1 if strict else 0)
    scores = jnp.where(mask, scores, 0.0)
    o_intra = jnp.einsum('bnhij,bnjhv->bnihv', scores, v)
    q_in = jnp.moveaxis(q * jnp.exp(b), 1, 0)
    k_st = jnp.moveaxis(k * jnp.exp(b_last - b), 1, 0)
    v_st = jnp.moveaxis(v, 1, 0)
    decay = jnp.moveaxis(jnp.exp(b_last[:, :, 0]), 1, 0)

    def step(state, xs):
        qc, kc, vc, dc = xs
        o = jnp.einsum('bihd,bhdv->bihv', qc, state)
        state = dc[..., None] * state + jnp.einsum('bjhd,bjhv->bhdv', kc, vc)
        return state, o

    state0 = jnp.zeros((B, H, DK, DV), f32)
    _, o_inter = lax.scan(step, state0, (q_in, k_st, v_st, decay))
    o = o_intra + jnp.moveaxis(o_inter, 0, 1)
    return o.reshape(B, S, H, DV)

def gla_branch(q, k, v, r, a_low, fgate_up, fgate_bias, out_norm):
    B, S, _ = q.shape
    q = q.reshape(B, S, GLA_HEADS, GLA_DK)
    k = k.reshape(B, S, GLA_HEADS, GLA_DK)
    v = v.reshape(B, S, GLA_HEADS, GLA_DV)
    a_low = a_low.reshape(B, S, 2, GLA_RANK)
    z = jnp.einsum('bsdr,drk->bsdk', a_low, fgate_up) + fgate_bias
    g = (jax.nn.log_sigmoid(z.astype(jnp.float32)) / GLA_TAU).reshape(B, S, 2, GLA_HEADS, GLA_DK)
    o_fwd = gla_chunked(q, k, v, g[:, :, 0], strict=False)
    o_bwd = jnp.flip(gla_chunked(jnp.flip(q, 1), jnp.flip(k, 1), jnp.flip(v, 1),
                                 jnp.flip(g[:, :, 1], 1), strict=True), 1)
    o = o_fwd + o_bwd
    o = o * lax.rsqrt(jnp.mean(o * o, axis=-1, keepdims=True) + EPS) * out_norm.astype(jnp.float32)
    y = o * jax.nn.silu(r.reshape(B, S, GLA_HEADS, GLA_DV).astype(jnp.float32))
    return y.reshape(B, S, GLA_V_W).astype(r.dtype)

def banded_attention(q, k, v, half):
    N, L, H, hd = q.shape
    nb = -(-L // half)
    Lp = nb * half
    padw = lambda t, lo, hi: jnp.pad(t, ((0, 0), (lo, hi), (0, 0), (0, 0)))
    qb = padw(q, 0, Lp - L).reshape(N, nb, half, H, hd).astype(jnp.float32)
    kp = padw(k, half, Lp - L + half).reshape(N, nb + 2, half, H, hd).astype(jnp.float32)
    vp = padw(v, half, Lp - L + half).reshape(N, nb + 2, half, H, hd).astype(jnp.float32)
    kb = jnp.concatenate([kp[:, :-2], kp[:, 1:-1], kp[:, 2:]], axis=2)
    vb = jnp.concatenate([vp[:, :-2], vp[:, 1:-1], vp[:, 2:]], axis=2)
    s = jnp.einsum('nbihd,nbjhd->nbhij', qb, kb) * (hd ** -0.5)
    qpos = jnp.arange(nb)[:, None] * half + jnp.arange(half)[None, :]
    kpos = jnp.arange(nb)[:, None] * half - half + jnp.arange(3 * half)[None, :]
    valid = ((jnp.abs(qpos[:, :, None] - kpos[:, None, :]) <= half)
             & (kpos[:, None, :] >= 0) & (kpos[:, None, :] < L))
    s = jnp.where(valid[None, :, None], s, -jnp.inf)
    m = jnp.max(s, axis=-1, keepdims=True)
    pr = jnp.exp(s - m)
    l = jnp.sum(pr, axis=-1, keepdims=True)
    o = jnp.einsum('nbhij,nbjhd->nbihd', pr / l, vb).reshape(N, Lp, H, hd)[:, :L]
    lse = jnp.transpose((m + jnp.log(l))[..., 0], (0, 1, 3, 2)).reshape(N, Lp, H)[:, :L]
    return o, lse

def dilated_group(q, k, v, window, dilation):
    B, S, H, hd = q.shape
    L = S // dilation
    half = window // (2 * dilation)
    to_sub = lambda t: t.reshape(B, L, dilation, H, hd).transpose(0, 2, 1, 3, 4).reshape(B * dilation, L, H, hd)
    o, lse = banded_attention(to_sub(q), to_sub(k), to_sub(v), half)
    o = o.reshape(B, dilation, L, H, hd).transpose(0, 2, 1, 3, 4).reshape(B, S, H, hd)
    lse = lse.reshape(B, dilation, L, H).transpose(0, 2, 1, 3).reshape(B, S, H)
    return o, lse

def dilated_branch(q, k, v, positions):
    B, S, _ = q.shape
    shp = (B, S, ATT_HEADS, ATT_HEAD_DIM)
    q = partial_rotary(q.reshape(shp), positions)
    k = partial_rotary(k.reshape(shp), positions)
    v = v.reshape(shp)
    outs, lses = [], []
    for gi, (window, dilation) in enumerate(ATT_GROUPS):
        hs = slice(gi * ATT_HEADS_PER_GROUP, (gi + 1) * ATT_HEADS_PER_GROUP)
        o, lse = dilated_group(q[:, :, hs], k[:, :, hs], v[:, :, hs], window, dilation)
        outs.append(o)
        lses.append(lse)
    w = jax.nn.softmax(jnp.stack(lses, axis=0), axis=0)
    o = jnp.sum(w[..., None] * jnp.stack(outs, axis=0), axis=0)
    return o.reshape(B, S, ATT_OUT_W).astype(q.dtype)

def moe(h, router_w, router_b, w1, b1, w2, b2):
    B, S, D = h.shape
    t = h.reshape(B * S, D)
    logits = (t @ router_w + router_b).astype(jnp.float32)
    top_val, top_idx = lax.top_k(logits, TOP_K)
    top_w = jax.nn.softmax(top_val, axis=-1)
    gates = jnp.sum(jax.nn.one_hot(top_idx, N_EXPERTS, dtype=jnp.float32) * top_w[..., None], axis=1)
    y = jnp.zeros((B * S, D), jnp.float32)
    for e in range(N_EXPERTS):
        hid = t @ w1[e] + b1[e]
        gate = jnp.minimum(hid[:, 0::2], SWIGLU_LIMIT)
        up = jnp.clip(hid[:, 1::2], -SWIGLU_LIMIT, SWIGLU_LIMIT)
        glu = gate * jax.nn.sigmoid(gate * SWIGLU_ALPHA)
        out = ((up + 1.0) * glu) @ w2[e] + b2[e]
        y = y + gates[:, e:e + 1] * out.astype(jnp.float32)
    return y.reshape(B, S, D).astype(h.dtype)

def setup_inputs(seed: int = 0) -> dict:
    key = jax.random.key(seed)
    ks = jax.random.split(key, 24)
    f32 = jnp.float32
    nrm = lambda kk, shape, scale: jax.random.normal(kk, shape, f32) * scale
    gain = lambda kk, shape: 1.0 + 0.02 * jax.random.normal(kk, shape, f32)
    return {
        'x': nrm(ks[0], (BATCH, SEQ, D_MODEL), 1.0),
        'p': nrm(ks[1], (DEPTH, BATCH, SEQ, PLE_DIM), 1.0),
        'positions': jnp.tile(jnp.arange(SEQ, dtype=jnp.int32)[None, :], (BATCH, 1)),
        'norm_mix': gain(ks[2], (DEPTH, D_MODEL)),
        'w_in': nrm(ks[3], (DEPTH, D_MODEL, IN_COLS), D_MODEL ** -0.5),
        'gla_fgate_up': nrm(ks[4], (DEPTH, 2, GLA_RANK, GLA_QK_W), GLA_RANK ** -0.5),
        'gla_fgate_bias': nrm(ks[5], (DEPTH, 2, GLA_QK_W), 0.1),
        'gla_out_norm': gain(ks[6], (DEPTH, GLA_HEADS, GLA_DV)),
        'w_branch_gla': nrm(ks[7], (DEPTH, GLA_V_W, D_MODEL), GLA_V_W ** -0.5),
        'w_branch_attn': nrm(ks[8], (DEPTH, ATT_OUT_W, D_MODEL), ATT_OUT_W ** -0.5),
        'w_out': nrm(ks[9], (DEPTH, D_MODEL, D_MODEL), D_MODEL ** -0.5),
        'norm_ffn': gain(ks[10], (DEPTH, D_MODEL)),
        'router_w': nrm(ks[11], (DEPTH, D_MODEL, N_EXPERTS), D_MODEL ** -0.5),
        'router_b': nrm(ks[12], (DEPTH, N_EXPERTS), 0.01),
        'expert_w1': nrm(ks[13], (DEPTH, N_EXPERTS, D_MODEL, 2 * D_EXPERT), D_MODEL ** -0.5),
        'expert_b1': nrm(ks[14], (DEPTH, N_EXPERTS, 2 * D_EXPERT), 0.01),
        'expert_w2': nrm(ks[15], (DEPTH, N_EXPERTS, D_EXPERT, D_MODEL), D_EXPERT ** -0.5),
        'expert_b2': nrm(ks[16], (DEPTH, N_EXPERTS, D_MODEL), 0.01),
        'norm_ple': gain(ks[17], (DEPTH, D_MODEL)),
        'ple_gate_w': nrm(ks[18], (DEPTH, D_MODEL, D_MODEL), D_MODEL ** -0.5),
        'ple_proj': nrm(ks[19], (DEPTH, PLE_DIM, D_MODEL), PLE_DIM ** -0.5),
        'norm_final': gain(ks[20], (D_MODEL,)),
    }

def reference(x, p, positions, norm_mix, w_in, gla_fgate_up, gla_fgate_bias, gla_out_norm,
              w_branch_gla, w_branch_attn, w_out, norm_ffn, router_w, router_b,
              expert_w1, expert_b1, expert_w2, expert_b2, norm_ple, ple_gate_w, ple_proj, norm_final):
    split_at = []
    acc = 0
    for width in IN_SPLITS[:-1]:
        acc += width
        split_at.append(acc)
    for i in range(DEPTH):
        h = rmsnorm(x, norm_mix[i])
        proj = h @ w_in[i]
        q_g, k_g, v_g, r_g, a_low, q_a, k_a, v_a, gate_a, gate_b = jnp.split(proj, split_at, axis=-1)
        y_gla = gla_branch(q_g, k_g, v_g, r_g, a_low, gla_fgate_up[i], gla_fgate_bias[i], gla_out_norm[i])
        y_att = dilated_branch(q_a, k_a, v_a, positions)
        merged = (jax.nn.sigmoid(gate_a) * (y_gla @ w_branch_gla[i])
                  + jax.nn.sigmoid(gate_b) * (y_att @ w_branch_attn[i]))
        x = x + merged @ w_out[i]
        x = x + moe(rmsnorm(x, norm_ffn[i]), router_w[i], router_b[i],
                    expert_w1[i], expert_b1[i], expert_w2[i], expert_b2[i])
        x = x + jax.nn.sigmoid(rmsnorm(x, norm_ple[i]) @ ple_gate_w[i]) * (p[i] @ ple_proj[i])
    return rmsnorm(x, norm_final)


_drawn_inputs = setup_inputs


def setup_inputs(seed=0):
    import zlib

    import numpy as np

    out = dict(_drawn_inputs(seed))
    spreads = {}
    factors = {'gla_out_norm': 3.437,
     'expert_b1': 8.0,
     'expert_b2': 8.0,
     'norm_ple': 152.118,
     'norm_final': 25.695}
    for name, (base, spread) in spreads.items():
        noise = np.random.default_rng([zlib.crc32(name.encode()), seed]).standard_normal(out[name].shape)
        drawn = base * np.exp(spread * noise) if base else spread * noise
        out[name] = jnp.asarray(drawn.astype(out[name].dtype))
    for name, factor in factors.items():
        out[name] = (out[name] * factor).astype(out[name].dtype)
    return out
```

```python
from contextlib import ExitStack
import math

import numpy as np
import concourse.bass as bass
from concourse import mybir

F32 = mybir.dt.float32
BF16 = mybir.dt.bfloat16
I32 = mybir.dt.int32
U32 = mybir.dt.uint32
ALU = mybir.AluOpType
ACT = mybir.ActivationFunctionType
AX = mybir.AxisListType.X

P = 128
D = 1024
SEQ = 256
NT = SEQ // P
KC = D // P
EPS = 1e-6
BANK = 512

GH, DK, DV = 4, 128, 256
RANK = 16
TAU = 16.0
CH = 64
NCH = SEQ // CH
AH, HD, GROUPS = 4, 64, 3
AHEADS = AH * GROUPS
AW = AHEADS * HD
ROT = HD // 4
HALF = ROT // 2
THETA = 500000.0
NEG = -1e30
PLE = 256
NE, TOPK = 32, 4
CAP = 64
PAIRS = NE // 2
PASSES = SEQ // CAP
ALPHA, LIMIT = 1.702, 7.0
WSLOTS = 12

C_Q, C_K = 0, GH * DK
C_V = C_K + GH * DK
C_R = C_V + GH * DV
C_LOW = C_R + GH * DV
C_QA = C_LOW + 2 * RANK
C_VA = C_QA + 2 * AW
C_GA = C_VA + AW
C_GB = C_GA + D
SLABS = [(C_LOW, 2 * RANK, True), (C_Q, 512, True), (C_K, 512, True), (C_V, 512, False), (C_V + 512, 512, False),
         (C_QA, 512, False), (C_QA + 512, 512, False), (C_QA + 1024, 512, False),
         (C_VA, 512, False), (C_VA + 512, AW - 512, False), (C_R, 512, False), (C_R + 512, 512, False),
         (C_GA, 512, True), (C_GA + 512, 512, True), (C_GB, 512, True), (C_GB + 512, 512, True)]
DVE_SLABS = (0, 3, 4, 8, 9, 10, 11)


def emptied(i):
    mine = i in DVE_SLABS
    return mine, sum((j in DVE_SLABS) == mine for j in range(i + 1))


def build(nc, x, p, positions, norm_mix, w_in, fgate_up, fgate_bias, out_norm, w_gla, w_att, w_out, norm_ffn,
          router_w, router_b, w1, b1, w2, b2, norm_ple, ple_gate_w, ple_proj, norm_final, out):
    with ExitStack() as ctx:
        def sb(name, shape, dt=F32):
            return ctx.enter_context(nc.sbuf_tensor(name, shape, dt))

        def sem(name):
            return ctx.enter_context(nc.semaphore(name))

        RING = sb("RING", [P, WSLOTS, 2048])
        ringf = RING[:, :, :].rearrange("p s n -> p (s n)")
        AREA = sb("AREA", [P, 96 * 256])

        def at(kib, n):
            return AREA[:, kib * 256:kib * 256 + n]

        def slot(i, n, base=0):
            return ringf[:, i * 2048 + base:i * 2048 + base + n]

        SLAB = [slot(8 + 2 * b, 4096).rearrange("p (k n) -> p k n", k=KC) for b in range(2)]
        W_OUT = slot(8, KC * D).rearrange("p (k n) -> p k n", k=KC)
        W_A = slot(0, KC * D).rearrange("p (k n) -> p k n", k=KC)
        DH = 2 * GH
        G_B0 = slot(0, 2048)
        G_B1 = slot(1, 2048)
        QT_ = slot(2, 2048)
        KT_ = slot(3, 2048)
        QIN = slot(4, 2048)
        KST = slot(5, 2048)
        G_E = slot(6, 2048)
        G_D = slot(7, 2048)
        RESET = slot(4, DH // 2 * SEQ)
        IOT = slot(5, 2 * 256).bitcast(I32).rearrange("p (t j) -> p t j", t=2)
        IOT2 = slot(5, 2 * 256, 512).bitcast(I32).rearrange("p (t j) -> p t j", t=2)
        KSTOK = G_E.rearrange("p (t f) -> p t f", t=NT)
        b3 = lambda v: v.rearrange("p (f s) -> p f s", s=SEQ)
        STATE = [G_D[:, i * DV:(i + 1) * DV] for i in range(8)] + [G_B0[:, i * DV:(i + 1) * DV] for i in range(8)] \
            + [G_B1[:, i * DV:(i + 1) * DV] for i in range(8)]
        QKAT = slot(4, 12 * SEQ).rearrange("p (c s) -> p c s", s=SEQ)
        SCO = [slot(4, 768, 3072), slot(4, 768, 3840)]
        PROB = [slot(4, 768, 4608), slot(4, 768, 5376)]
        PT = slot(4, 6 * SEQ, 6144).rearrange("p (c s) -> p c s", s=SEQ)

        YAT = slot(4, 2 * SEQ, 7680).rearrange("p (c s) -> p c s", s=SEQ)

        X = at(0, 2048).rearrange("p (t d) -> p t d", t=NT)
        H = at(8, 2048).rearrange("p (t d) -> p t d", t=NT)
        HT = at(16, 2048).rearrange("p (k s) -> p k s", k=KC)
        QK_T = at(24, 2048)
        YT = at(24, 2048).rearrange("p (k s) -> p k s", k=KC)
        V = at(32, 2048).rearrange("p (t d) -> p t d", t=NT)
        R = at(40, 2048).rearrange("p (t d) -> p t d", t=NT)
        GA = at(48, 2048).rearrange("p (k s) -> p k s", k=KC)
        GB = at(56, 2048).rearrange("p (k s) -> p k s", k=KC)
        QKA = at(64, 3072).rearrange("p (t f) -> p t f", t=NT)
        VA = at(76, 1536).rearrange("p (t f) -> p t f", t=NT)
        AM = at(82, 1536).bitcast(I32).rearrange("p (t j) -> p t j", t=NT)
        W_B = at(88, 2048).rearrange("p (k n) -> p k n", k=2)
        ROTB = [at(8 + 2 * i, 384).rearrange("p (t h j) -> p t h j", t=NT, j=HALF) for i in range(4)]
        JUNK = at(16, 2048)
        YJUNK = at(8, 2048)
        W_G = at(32, KC * D).rearrange("p (k n) -> p k n", k=KC)
        B1S = at(40, 2048)
        B1P = at(64, 1024).bitcast(BF16)
        HTE = at(68, 1024).rearrange("p (k s) -> p k s", k=KC)
        GT = at(72, 512).rearrange("p (e t s) -> p e t s", e=2, t=NT)
        GD = at(74, 512).rearrange("p (e t f) -> p e t f", e=2, t=NT)
        GATE, SIG, UP = at(76, 512), at(78, 512), at(80, 512)
        HITS = at(76, NT * TOPK * NE)
        A, AT, OUTE = at(82, 512), at(84, 512), at(86, 512)
        PTOK = at(84, 512).rearrange("p (t d) -> p t d", t=NT)
        PTT = at(86, 512).rearrange("p (k s) -> p k s", k=2)
        PP = at(88, 2048).rearrange("p (t d) -> p t d", t=NT)
        W_P = at(24, 2048).rearrange("p (k n) -> p k n", k=2)
        NF = at(24, 1024)
        LPART = at(82, SEQ)
        ONEHOT = sb("ONEHOT", [P, NT, 2, CAP])

        IDENT = sb("IDENT", [P, P])
        ONES = sb("ONES", [P, P])
        TRI = sb("TRI", [P, P])
        MF = sb("MF", [P, CH])
        MB = sb("MB", [P, CH])
        IOS = sb("IOS", [P, CAP])
        IO32 = sb("IO32", [P, NE])
        UB = sb("UB", [NE, D])
        VEC = slot(6, P)[0:40, :]
        COL = sb("COL", [P, 40])
        RW = sb("RW", [P, KC, NE])
        RB = sb("RB", [1, NE])
        RBB = sb("RBB", [P, NE])
        SEL4 = sb("SEL4", [P, NE])
        LOWT = sb("LOWT", [2 * RANK, SEQ])
        DEC = sb("DEC", [P, DH * NCH])
        ST = sb("ST", [P, 512])
        SS = sb("SS", [P, 16])
        POSI = sb("POSI", [P, NT], I32)
        POSF = sb("POSF", [P, NT])
        INVF = sb("INVF", [P, HALF])
        ANG = sb("ANG", [P, 2, NT * HALF])
        TRN = sb("TRN", [P, 2, NT * HALF])
        TURN_I = sb("TURN_I", [P, 2, NT * HALF], I32)
        CS = sb("CS", [P, 2, NT * HALF])
        MX = sb("MX", [P, 4 * 8])
        LOG = sb("LOG", [P, NT, NE])
        TOP = sb("TOP", [P, NT, 8])
        TOPI = sb("TOPI", [P, NT, 8], U32)
        TOPF = sb("TOPF", [P, NT, 8])
        TW = sb("TW", [P, NT, 8])
        GATES = sb("GATES", [P, NT, NE])
        SEL = sb("SEL", [P, NT, NE])
        RANKS = sb("RANKS", [P, NT, NE])
        GATT = sb("GATT", [NE, SEQ])
        CNT = sb("CNT", [P, 1])
        CNTI = sb("CNTI", [P, 1], I32)
        SELT = sb("SELT", [P, NE], BF16)
        SELE = sb("SELE", [P, 2, CAP], BF16)
        SELI = sb("SELI", [P, 2, NE], I32)

        PS = ctx.enter_context(nc.psum_tensor("PS", [P, 8, BANK], F32))

        def bank(i, n=BANK, base=0):
            return PS[:, i, base:base + n]

        def pair(i):
            return PS[:, i:i + 2, :].rearrange("p b n -> p (b n)")

        dve_step, act_step, pool_step = sem("dve_step"), sem("act_step"), sem("pool_step")
        x_in = [sem("x_in0"), sem("x_in1")]
        vec_in, small_in, pos_in = sem("vec_in"), sem("small_in"), sem("pos_in")
        slab_in = [sem("slab_in0"), sem("slab_in1")]
        wa_in, wb_in, wout_in, p_in, b1_in, b2_in = (sem(n) for n in ("wa_in", "wb_in", "wout_in", "p_in", "b1_in", "b2_in"))
        wg_in, nf_in, u_in, out_written = sem("wg_in"), sem("nf_in"), sem("u_in"), sem("out_written")
        u_zero, consts, iotas = sem("u_zero"), sem("consts"), sem("iotas")
        squares, h_ready, turned, turn_read = sem("squares"), sem("h_ready"), sem("turned"), sem("turn_read")
        inv_ready, rms_ready = sem("inverse_ready"), sem("rms_ready")
        vec_turned, cols_ready = sem("vec_turned"), sem("cols_ready")
        slab_done, slab_act, slab_dve, sil = sem("slab_done"), sem("slab_emptied_act"), sem("slab_emptied_dve"), sem("r_sigmoid")
        z_done, z_read, z_abs, lse_part, g_cum = sem("z_done"), sem("z_read"), sem("z_abs"), sem("z_log"), sem("g_cum")
        diff, expd, expd_used = sem("gla_diff"), sem("gla_exp"), sem("gla_exp_used")
        qt_ready, kst_ready, scores_done, st_ready = sem("qt_ready"), sem("kst_ready"), sem("gla_scores"), sem("st_ready")
        kst_turned, kstok_ready, kv_done, state_ready = sem("kst_turned"), sem("kstok_ready"), sem("kv_done"), sem("state_ready")
        o_done, o_sq, y_ready = sem("o_done"), sem("o_squares"), sem("y_ready")
        ang_ready, trig, rotated = sem("ang_ready"), sem("trig_ready"), sem("rotated")
        qka_turned, qkat_ready = sem("qka_turned"), sem("qkat_ready")
        att_s, att_masked, att_max, att_exp, att_prob = (sem(n) for n in ("att_scores", "att_masked", "att_max", "att_exp", "att_prob"))
        att_t, pt_ready, att_o, yat_ready = sem("att_turned"), sem("pt_ready"), sem("att_out"), sem("yat_ready")
        a_done, a_used, b_done, m_ready = sem("branch_a_done"), sem("branch_a_used"), sem("branch_b_done"), sem("merged")
        mix_done, x_mixed = sem("mix_done"), sem("x_mixed")
        p_turned, ptt_ready, pp_done, pp_ready = sem("p_turned"), sem("ptt_ready"), sem("pp_done"), sem("pp_ready")
        log_done, log_read, logits_max, top_exp = sem("log_done"), sem("log_read"), sem("top_ready"), sem("top_exp")
        sel_ready, rank_done, gatt_done, gatt_ready, b2_done = (sem(n) for n in ("sel_ready", "rank_done", "gatt_done", "gatt_ready", "b2_done"))
        flag_ready, b1p_ready, b2_added = sem("flag_ready"), sem("b1p_ready"), sem("b2_added")
        land = [sem(f"w_land{s}") for s in range(WSLOTS)]
        w_used = sem("w_used")
        onehot, gd_ready, tg_done, gt_ready = sem("onehot_ready"), sem("gd_ready"), sem("gd_turned"), sem("gt_ready")
        ga_done, ht_ready, hid_done, gate_in = sem("gathered"), sem("hte_ready"), sem("hid_done"), sem("gate_ready")
        hid_read, glu_part, sig_ready, a_ready = sem("hid_read"), sem("glu_part"), sem("sig_ready"), sem("a_ready")
        at_done, at_ready, oe_done, oe_ready = sem("a_turned"), sem("at_ready"), sem("expert_out"), sem("oute_ready")
        sc_done, x_added, pleg_done, ple_sig = sem("scattered"), sem("x_added"), sem("ple_gate_done"), sem("ple_sig")
        part_done, part_ready, gates_ready, fin_ready, x_final, sele_ready, ios_moved = sem("part_done"), sem("part_ready"), sem("gates_ready"), sem("fin_ready"), sem("x_final"), sem("sele_ready"), sem("ios_moved")

        def steps(eng, own):
            count = {}

            def step(ins, s=own):
                count[s.name] = count.get(s.name, 0) + 1
                ins.then_inc(s, 1)
                eng.wait_ge(s, count[s.name])
            return step

        def past(eng, s, n):
            if not isinstance(n, int) or n > 0:
                eng.wait_ge(s, n)

        def runtime_pass(eng, body):
            body(0)
            eng.wait_ge(flag_ready, 1)
            most = eng.value_load(CNTI[0:1, 0:1], min_val=0, max_val=SEQ)
            with eng.If(most > CAP):
                with eng.Fori(1, PASSES) as q:
                    body(q)
            eng.nop()

        block = ctx.enter_context(nc.Block())

        @block.sync
        def _(eng):
            for t in range(NT):
                eng.dma_start(X[:, t, :], x[0, t * P:(t + 1) * P, :]).then_inc(x_in[t], 16)

            def load_slab(i):
                c0, w, _ = SLABS[i]
                if i >= 2:
                    eng.wait_ge(slab_done, i - 1)
                eng.dma_start(SLAB[i % 2][:, :, 0:w], w_in[0, :, c0:c0 + w].rearrange("(k p) n -> p k n", p=P)
                              ).then_inc(slab_in[i % 2], 16)

            for i in range(12):
                load_slab(i)
            eng.dma_start(W_B, w_att[0].rearrange("(k p) n -> p k n", p=P)).then_inc(wb_in, 16)
            eng.wait_ge(z_done, 1)
            eng.dma_start(UB[:, :], b2[0]).then_inc(b2_in, 16)
            load_slab(12)
            load_slab(13)
            eng.wait_ge(y_ready, 8)
            eng.dma_start(W_A, w_gla[0].rearrange("(k p) n -> p k n", p=P)).then_inc(wa_in, 16)
            load_slab(14)
            eng.wait_ge(turned, 8)
            for r in range(3):
                eng.dma_start(B1S[32 * r:32 * r + 32, :], b1[0]).then_inc(b1_in, 16)
            load_slab(15)
            eng.wait_ge(slab_done, len(SLABS))
            eng.dma_start(W_OUT, w_out[0].rearrange("(k p) n -> p k n", p=P)).then_inc(wout_in, 16)
            eng.wait_ge(a_done, 4)
            eng.dma_start(W_P, ple_proj[0].rearrange("(k p) n -> p k n", p=P)).then_inc(p_in, 16)
            eng.wait_ge(b_done, 4)
            eng.dma_start(PTOK, p[0, 0].rearrange("(t p) d -> p t d", p=P)).then_inc(p_in, 16)

            def load_expert(e, slots):
                for s in slots:
                    if s < 8:
                        eng.dma_start(RING[:, s, :], w1[0, e, s * P:(s + 1) * P, :]).then_inc(land[s], 16)
                    else:
                        eng.dma_start(RING[:, s, :].rearrange("p (a n) -> p a n", a=2),
                                      w2[0, e, (s - 8) * 2 * P:(s - 7) * 2 * P, :].rearrange("(a p) n -> p a n", p=P)
                                      ).then_inc(land[s], 16)

            load_expert(0, range(0, 8))
            eng.wait_ge(mix_done, 4)
            load_expert(0, range(8, WSLOTS))
            eng.wait_ge(b1p_ready, 3)
            eng.dma_start(W_G, ple_gate_w[0].rearrange("(k p) n -> p k n", p=P)).then_inc(wg_in, 16)

            def experts(q):
                first = 1 if isinstance(q, int) else 0
                with eng.Fori(first, NE) as e:
                    for s in range(WSLOTS):
                        n = q * NE + e
                        if s == 7:
                            eng.wait_ge(hid_done, n)
                        elif s == WSLOTS - 1:
                            eng.wait_ge(oe_done, n)
                        else:
                            eng.wait_ge(w_used, (n - 1) * (WSLOTS - 2) + (s + 1 if s < 7 else s))
                        load_expert(e, [s])

            eng.wait_ge(pp_ready, 2)
            eng.dma_start(NF, norm_final.rearrange("(a n) -> a n", a=1).to_broadcast([P, D])).then_inc(nf_in, 16)
            runtime_pass(eng, experts)
            for t in range(NT):
                eng.wait_ge(fin_ready, t + 1)
                eng.dma_start(out[0, t * P:(t + 1) * P, :], X[:, t, :]).then_inc(out_written, 16)
            eng.wait_ge(out_written, 16 * NT)

        @block.gpsimd
        def _(eng):
            step = steps(eng, pool_step)
            step(eng.memset(UB[:, :], 0.0), u_zero)
            step(eng.memset(IDENT[:, :], 0.0))
            step(eng.memset(ONES[:, :], 1.0))
            step(eng.memset(TRI[:, :], 1.0))
            step(eng.memset(MF[:, :], 1.0))
            step(eng.memset(MB[:, :], 1.0))
            step(eng.affine_select(out=IDENT[:, :], in_=IDENT[:, :], compare_op=ALU.not_equal, fill=1.0, base=0,
                                   pattern=[[-1, P]], channel_multiplier=1))
            step(eng.affine_select(out=TRI[:, :], in_=TRI[:, :], compare_op=ALU.is_gt, fill=0.0, base=0,
                                   pattern=[[1, P]], channel_multiplier=-1))
            for h in range(2):
                rows = slice(CH * h, CH * h + CH)
                step(eng.affine_select(out=MF[rows, :], in_=MF[rows, :], compare_op=ALU.is_ge, fill=0.0, base=0,
                                       pattern=[[1, CH]], channel_multiplier=-1))
                step(eng.affine_select(out=MB[rows, :], in_=MB[rows, :], compare_op=ALU.is_gt, fill=0.0, base=0,
                                       pattern=[[-1, CH]], channel_multiplier=1))
            step(eng.iota(IOS[:, :], pattern=[[1, CAP]], base=1, channel_multiplier=0, allow_small_or_imprecise_dtypes=True))
            step(eng.iota(IO32[:, :], pattern=[[1, NE]], base=0, channel_multiplier=0, allow_small_or_imprecise_dtypes=True))
            step(eng.iota(IOT, pattern=[[-P, NT], [1, SEQ]], base=0, channel_multiplier=-1))
            step(eng.iota(SELI[:, 0, :], pattern=[[-1, NE]], base=NE, channel_multiplier=1), iotas)
            eng.wait_ge(b1_in, 48)
            eng.wait_ge(qka_turned, 6)
            step(eng.memset(B1P, 0.0))
            for r in range(3):
                rows = slice(32 * r, 32 * r + 32)
                for part in range(r + 1):
                    step(eng.tensor_copy(B1P[rows, :], B1S[rows, :]), b1p_ready if part == r else pool_step)
                    if part < r:
                        step(eng.tensor_tensor(B1S[rows, :], B1S[rows, :], B1P[rows, :], ALU.subtract))

        @block.scalar
        def _(eng):
            step = steps(eng, act_step)
            act = eng.activation

            def sum_squares(col, junk, n, ready=None):
                step(act(MX[:, 31:32], ONES[:, 0:1], ACT.Sqrt))
                for t in range(NT):
                    if ready:
                        eng.wait_ge(*ready[t])
                    step(act(junk[:, t * D:(t + 1) * D], X[:, t, :], ACT.Square, accum_out=SS[:, col + t:col + t + 1]), squares)
                eng.wait_ge(inv_ready, n)
                step(act(SS[:, col:col + NT], SS[:, col:col + NT], ACT.Sqrt), rms_ready)

            for i, v in enumerate((norm_mix[0], norm_ffn[0], norm_ple[0], out_norm[0].rearrange("a b -> (a b)"),
                                   fgate_bias[0].rearrange("a b -> (a b)"))):
                eng.dma_start(VEC[8 * i:8 * i + 8, :], v.rearrange("(k p) -> k p", p=P)).then_inc(vec_in, 16)
            eng.wait_ge(iotas, 1)
            sum_squares(0, JUNK, 1, [(x_in[t], 16) for t in range(NT)])
            with nc.allow_non_contiguous_dma(reason="256 positions"):
                eng.dma_start(POSI[:, :], positions[0].rearrange("(t p) -> p t", p=P)).then_inc(pos_in, 16)
            eng.wait_ge(u_zero, 1)
            for d in range(2):
                eng.dma_start(UB[RANK * d:RANK * d + RANK, 512 * d:512 * d + 512], fgate_up[0, d]).then_inc(u_in, 16)
            eng.dma_start(RW[:, :, :], router_w[0].rearrange("(k p) n -> p k n", p=P)).then_inc(small_in, 16)
            eng.dma_start(RB[:, :], router_b).then_inc(small_in, 16)
            eng.wait_ge(ang_ready, 1)
            step(act(CS[:, :, :], ANG[:, :, :], ACT.Sin), trig)

            def slab_banks(i):
                eng.wait_ge(slab_done, i + 1)
                return 2 * (i % 2)

            b = slab_banks(1)
            step(act(QK_T[:, 0:1024], pair(b), ACT.Copy, scale=float(DK) ** -0.5), slab_act)
            b = slab_banks(2)
            step(act(QK_T[:, 1024:2048], pair(b), ACT.Copy), slab_act)
            eng.wait_ge(z_done, 1)
            for c in range(8):
                ins = act(G_B0[:, c * SEQ:(c + 1) * SEQ], bank(4 + c // 2, SEQ, c % 2 * SEQ), ACT.Identity,
                          bias=COL[:, 32 + c:33 + c])
            step(ins, z_read)
            step(act(G_B1, G_B0, ACT.Abs))
            step(act(G_B1, G_B1, ACT.Exp, scale=-1.0))
            step(act(G_B1, G_B1, ACT.Ln, bias=1.0), lse_part)
            eng.wait_ge(diff, 1)
            step(act(G_E, G_D, ACT.Exp, scale=1 / TAU), expd)
            step(act(G_B0, G_D, ACT.Exp, scale=-1 / TAU), expd)
            eng.wait_ge(expd_used, 1)
            step(act(G_E, G_B1, ACT.Exp, scale=1 / TAU), expd)
            eng.wait_ge(diff, 2)
            step(act(G_B0, G_D, ACT.Exp, scale=1 / TAU), expd)
            gb = G_B1.rearrange("p (f c i) -> p f c i", c=NCH, i=CH)
            decv = DEC[:, :].rearrange("p (f c) -> p f c", c=NCH)
            step(act(decv[:, 0:GH, :], gb[:, 0:GH, :, CH - 1], ACT.Exp, scale=1 / TAU), expd)
            step(act(decv[:, GH:, :], gb[:, GH:, :, 0], ACT.Exp, scale=1 / TAU), expd)
            for i in (5, 6, 7):
                b = slab_banks(i)
                for t in range(NT):
                    ins = act(QKA[:, t, (i - 5) * 512:(i - 4) * 512], bank(b + t), ACT.Copy)
                step(ins, slab_act)
            for n in range(4):
                t, d = n // 2, n % 2
                eng.wait_ge(kst_turned, n + 1)
                if n == 0:
                    eng.wait_ge(expd_used, 2)
                step(act(KSTOK[:, t, d * 512:d * 512 + 512], bank(6 + n % 2), ACT.Copy), kstok_ready)
            for i in (10, 11):
                b = slab_banks(i)
                for t in range(NT):
                    ins = act(R[:, t, (i - 10) * 512:(i - 9) * 512], bank(b + t), ACT.Sigmoid)
                step(ins, sil)
            eng.wait_ge(o_done, 1)
            for t in range(NT):
                for h in range(GH):
                    step(act(YJUNK[:, 0:DV], PS[:, 4 + 2 * t + h // 2, h % 2 * DV:h % 2 * DV + DV], ACT.Square,
                             accum_out=SS[:, 4 + GH * t + h:5 + GH * t + h]), o_sq)
            eng.wait_ge(inv_ready, 2)
            step(act(SS[:, 4:4 + NT * GH], SS[:, 4:4 + NT * GH], ACT.Sqrt), rms_ready)
            b = slab_banks(12)
            step(act(GA[:, 0:4, :].rearrange("p k s -> p (k s)"), pair(b), ACT.Sigmoid), slab_act)
            for n in range(6):
                eng.wait_ge(qka_turned, n + 1)
                step(act(QKAT[:, 2 * n:2 * n + 2, :].rearrange("p c s -> p (c s)"), bank(4 + n % 4), ACT.Copy), qkat_ready)

            def gates_a(i):
                b = slab_banks(i)
                dst = (GA, GA, GB, GB)[i - 12][:, 4 * (i % 2):4 * (i % 2) + 4, :]
                step(act(dst.rearrange("p k s -> p (k s)"), pair(b), ACT.Sigmoid), slab_act)

            def soft(h):
                for t in range(NT):
                    u = NT * h + t
                    eng.wait_ge(att_max, u + 1)
                    if h:
                        eng.wait_ge(att_t, u - 1)
                    step(act(PROB[t], SCO[t], ACT.Exp, scale=HD ** -0.5, bias=MX[:, 8 + u:9 + u],
                             accum_out=MX[:, 16 + u:17 + u]), att_exp)

            def pt_copy(h):
                for t in range(NT):
                    eng.wait_ge(att_t, NT * h + t + 1)
                    if h and t == 0:
                        eng.wait_ge(att_o, h)
                    src = PS[:, 4 + 2 * t:6 + 2 * t, :].rearrange("p b n -> p (b n)")[:, 0:768]
                    step(act(PT[:, :, t * P:(t + 1) * P], src.rearrange("p (c i) -> p c i", i=P), ACT.Copy), pt_ready)

            soft(0)
            gates_a(13)
            pt_copy(0)
            gates_a(14)
            soft(1)
            gates_a(15)
            pt_copy(1)
            soft(2)
            pt_copy(2)
            soft(3)
            pt_copy(3)
            eng.wait_ge(p_turned, 1)
            step(act(PTT.rearrange("p k s -> p (k s)"), bank(0), ACT.Copy), ptt_ready)
            sum_squares(2, YJUNK, 3, [(x_mixed, 2), (x_mixed, 4)])
            eng.wait_ge(logits_max, 1)
            for t in range(NT):
                ins = act(TW[:, t, 0:TOPK], TOP[:, t, 0:TOPK], ACT.Exp, bias=MX[:, t:t + 1], accum_out=MX[:, 2 + t:3 + t])
            step(ins, top_exp)
            for t in range(NT):
                eng.wait_ge(pp_done, t + 1)
                step(act(PP[:, t, :], pair(6 * t), ACT.Copy), pp_ready)

            def sigmoid(n):
                eng.wait_ge(gate_in, n)
                past(eng, a_ready, n - 1)
                act(SIG, GATE, ACT.Sigmoid, scale=ALPHA).then_inc(sig_ready, 1)

            def a_copy(n):
                eng.wait_ge(at_done, n)
                past(eng, oe_done, n - 1)
                act(AT, bank(5), ACT.Copy).then_inc(at_ready, 1)

            def out_copy(n):
                eng.wait_ge(oe_done, n)
                past(eng, sc_done, 2 * n - 2)
                act(OUTE, bank(4), ACT.Copy).then_inc(oe_ready, 1)

            def moe(q):
                def one(i):
                    n = (q * PAIRS + i) * 2
                    sigmoid(n + 1)
                    eng.wait_ge(tg_done, q * PAIRS + i + 1)
                    past(eng, sc_done, 2 * n)
                    act(GT.rearrange("p e t s -> p (e t s)"), bank(4), ACT.Copy).then_inc(gt_ready, 1)
                    a_copy(n + 1)
                    out_copy(n + 1)
                    sigmoid(n + 2)
                    a_copy(n + 2)
                    out_copy(n + 2)

                one(0)
                with eng.Fori(1, PAIRS) as i:
                    one(i)

            runtime_pass(eng, moe)
            eng.wait_ge(x_final, 1)
            sum_squares(12, YJUNK, 4)
            for t in range(NT):
                for c in range(2):
                    n = 2 * t + c
                    eng.wait_ge(pleg_done, n + 1)
                    step(act(H[:, t, c * 512:c * 512 + 512], bank(n), ACT.Sigmoid, scale=SS[:, 12 + t:13 + t]), ple_sig)
                eng.wait_ge(x_final, 2 + t)
                step(act(H[:, t, :], X[:, t, :], ACT.Square, accum_out=SS[:, 14 + t:15 + t]), squares)
                eng.wait_ge(inv_ready, 5 + t)
                step(act(SS[:, 14 + t:15 + t], SS[:, 14 + t:15 + t], ACT.Sqrt), rms_ready)

        @block.vector
        def _(eng):
            step = steps(eng, dve_step)
            tt, ts, stt = eng.tensor_tensor, eng.tensor_scalar, eng.scalar_tensor_tensor

            def invert(s, n):
                step(ts(s, s, 1.0 / n, EPS, ALU.mult, ALU.add))
                step(eng.reciprocal(s, s), inv_ready)
                inverted[0] += 1
                eng.wait_ge(rms_ready, inverted[0])

            inverted = [0]

            def normed(col):
                invert(SS[:, col:col + NT], D)
                for t in range(NT):
                    step(ts(H[:, t, :], X[:, t, :], SS[:, col + t:col + t + 1], None, ALU.mult), h_ready)

            def turn_copy(use, dst, col):
                for j in range(4):
                    eng.wait_ge(turned, 4 * use + j + 1)
                    step(tt(dst[:, 2 * j:2 * j + 2, :], bank(4 + j).rearrange("p (c s) -> p c s", c=2),
                            COL[:, col + 2 * j:col + 2 * j + 2].unsqueeze(2).broadcast_to([P, 2, SEQ]), ALU.mult), turn_read)

            for j in range(HALF):
                ins = eng.memset(INVF[:, j:j + 1], float(np.float32(THETA) ** np.float32(-2.0 * j / ROT)))
            step(ins)
            for t in range(NT):
                eng.wait_ge(x_in[t], 16)
            eng.wait_ge(squares, 2)
            normed(0)
            eng.wait_ge(vec_turned, 1)
            step(eng.tensor_copy(COL[:, :], bank(7, 40)), cols_ready)
            turn_copy(0, HT, 0)
            eng.wait_ge(slab_done, 1)
            step(eng.tensor_copy(LOWT[:, :], PS[0:2 * RANK, 0, 0:SEQ]), slab_dve)
            eng.wait_ge(pos_in, 16)
            step(eng.tensor_copy(POSF[:, :], POSI[:, :]))
            for v in range(2):
                step(tt(ANG[:, v, :].rearrange("p (t j) -> p t j", j=HALF), POSF[:, :].unsqueeze(2).broadcast_to([P, NT, HALF]),
                        INVF[:, :].unsqueeze(1).broadcast_to([P, NT, HALF]), ALU.mult))
            two_pi = 2 * math.pi
            c1 = 6.28125
            c2 = float(np.float32((two_pi - c1) * 2 ** 20).astype(np.int32)) / 2 ** 20
            c3 = two_pi - c1 - c2
            for v, turn in ((0, 0.25), (1, 0.0)):
                step(ts(TRN[:, v, :], ANG[:, v, :], 1 / two_pi, turn, ALU.mult, ALU.add))
            step(eng.tensor_copy(TURN_I[:, :, :], TRN[:, :, :]))
            step(eng.tensor_copy(TRN[:, :, :], TURN_I[:, :, :]))
            for c in (c1, c2, c3):
                step(stt(out=ANG[:, :, :], in0=TRN[:, :, :], scalar=-c, in1=ANG[:, :, :], op0=ALU.mult, op1=ALU.add))
            step(ts(ANG[:, 0, :], ANG[:, 0, :], math.pi / 2, None, ALU.add))
            pi_in = float(np.nextafter(np.float32(math.pi), np.float32(0)))
            step(ts(ANG[:, :, :], ANG[:, :, :], pi_in, -pi_in, ALU.min, ALU.max), ang_ready)
            eng.wait_ge(iotas, 1)
            am = AM.rearrange("p t (g j) -> p t g j", g=GROUPS)
            step(tt(IOT2, IOT, IOT, ALU.mult))
            step(ts(am[:, :, 0, :], IOT2, 64.0 * 64.0, None, ALU.is_le))
            for g, dil in ((1, 4), (2, 16)):
                step(ts(IOT2, IOT, dil - 1, None, ALU.bitwise_and))
                step(ts(am[:, :, g, :], IOT2, 0.0, None, ALU.is_equal))
            step(eng.memset(SELT[:, :], 0.0))
            step(ts(SELI[:, 1, :], SELI[:, 0, :], NE - 1, None, ALU.bitwise_and))
            for r in range(3):
                step(ts(SELT[32 * r:32 * r + 32, :], SELI[32 * r:32 * r + 32, 1, :], 0.0, None, ALU.is_equal))
            step(ts(SEL4[:, :], SELI[:, 1, :], 0.0, None, ALU.is_equal))
            eng.wait_ge(lse_part, 1)
            step(eng.memset(RESET, 1.0))
            step(eng.memset(RESET.rearrange("p (c i) -> p c i", i=CH)[:, :, 0], 0.0))
            step(stt(out=G_B0, in0=G_B0, scalar=0.0, in1=G_B1, op0=ALU.min, op1=ALU.subtract))
            half = GH * SEQ
            step(eng.tensor_tensor_scan(G_B1[:, 0:half], RESET, G_B0[:, 0:half], 0.0, ALU.mult, ALU.add))
            step(eng.tensor_tensor_scan(G_B1[:, 2 * half - 1:half - 1:-1], RESET, G_B0[:, 2 * half - 1:half - 1:-1],
                                        0.0, ALU.mult, ALU.add), g_cum)

            def empty_to(i, dst):
                eng.wait_ge(slab_done, i + 1)
                w = SLABS[i][1]
                for t in range(NT):
                    ins = eng.tensor_copy(dst[:, t, :], bank(2 * (i % 2) + t, w))
                step(ins, slab_dve)

            chunks = lambda v, d: v[:, d * half:(d + 1) * half].rearrange("p (c i) -> p c i", i=CH)
            q2 = QK_T[:, 0:half].unsqueeze(1).broadcast_to([P, 2, half])
            k2 = QK_T[:, half:2 * half].unsqueeze(1).broadcast_to([P, 2, half])
            two = lambda v: v.rearrange("p (d f) -> p d f", d=2)

            def difference(refs, sign):
                for d in range(2):
                    b = chunks(G_B1, d)
                    ref = b[:, :, refs[d]:refs[d] + 1].broadcast_to([P, GH * NCH, CH])
                    x0, x1 = (b, ref) if sign > 0 else (ref, b)
                    ins = tt(chunks(G_D, d), x0, x1, ALU.subtract)
                step(ins, diff)

            difference((CH // 2 - 1, CH // 2), 1)
            empty_to(3, V[:, :, 0:512])
            eng.wait_ge(slab_act, 2)
            eng.wait_ge(expd, 1)
            step(tt(two(QT_), two(G_E), q2, ALU.mult), expd_used)
            eng.wait_ge(expd, 2)
            step(tt(two(KT_), two(G_B0), k2, ALU.mult), qt_ready)
            difference((CH - 1, 0), -1)
            empty_to(4, V[:, :, 512:1024])
            eng.wait_ge(expd, 3)
            step(tt(two(QIN), two(G_E), q2, ALU.mult), expd_used)
            eng.wait_ge(expd, 4)
            step(tt(two(KST), two(G_B0), k2, ALU.mult), kst_ready)
            eng.wait_ge(trig, 1)
            eng.wait_ge(slab_act, 5)
            heads = QKA.rearrange("p t (h e) -> p t h e", e=HD)
            for t in range(NT):
                t1, t2 = heads[:, t, :, 0:HALF], heads[:, t, :, HALF:ROT]
                cos, sin = (CS[:, v, t * HALF:(t + 1) * HALF].unsqueeze(1).broadcast_to([P, 2 * AHEADS, HALF]) for v in range(2))
                rb = [b[:, t] for b in ROTB]
                step(tt(rb[0], t1, cos, ALU.mult))
                step(tt(rb[1], t2, sin, ALU.mult))
                step(tt(rb[2], t2, cos, ALU.mult))
                step(tt(rb[3], t1, sin, ALU.mult))
                step(tt(t1, rb[0], rb[1], ALU.subtract))
                step(tt(t2, rb[2], rb[3], ALU.add), rotated)
            empty_to(8, VA[:, :, 0:512])
            eng.wait_ge(scores_done, 1)
            for m, i in ((MF, 4), (MB, 5)):
                step(eng.copy_predicated(ST[:, :].rearrange("p (f i) -> p f i", i=CH),
                                         m[:, :].bitcast(U32).unsqueeze(1).broadcast_to([P, 8, CH]),
                                         bank(i).rearrange("p (f i) -> p f i", i=CH)), st_ready)
            empty_to(9, VA[:, :, 512:768])
            for s in range(NCH - 1):
                for dh in range(DH):
                    d, h = dh // GH, dh % GH
                    eng.wait_ge(kv_done, 4 * s + dh // 2 + 1)
                    kv = bank(4 + dh // 2, DV, dh % 2 * DV)
                    if s == 0:
                        if dh == 0:
                            eng.wait_ge(expd, 6)
                            eng.wait_ge(kstok_ready, 4)
                        step(eng.tensor_copy(STATE[dh], kv), state_ready)
                    else:
                        c = s if d == 0 else NCH - 1 - s
                        step(stt(out=STATE[8 * s + dh], in0=STATE[8 * (s - 1) + dh],
                                 scalar=DEC[:, dh * NCH + c:dh * NCH + c + 1], in1=kv, op0=ALU.mult, op1=ALU.add), state_ready)
            for i in (10, 11):
                eng.wait_ge(sil, i - 9)
                for t in range(NT):
                    r = R[:, t, (i - 10) * 512:(i - 9) * 512]
                    ins = tt(r, r, bank(2 * (i % 2) + t), ALU.mult)
                step(ins, slab_dve)
            eng.wait_ge(o_sq, 2 * GH)
            invert(SS[:, 4:4 + NT * GH], DV)
            for t in range(NT):
                for h in range(GH):
                    r = R[:, t, h * DV:(h + 1) * DV]
                    step(stt(out=r, in0=PS[:, 4 + 2 * t + h // 2, h % 2 * DV:h % 2 * DV + DV],
                             scalar=SS[:, 4 + GH * t + h:5 + GH * t + h], in1=r, op0=ALU.mult, op1=ALU.mult), y_ready)
            turn_copy(1, YT, 24)

            for t in range(NT):
                step(eng.memset(SCO[t], NEG))

            def softmax_in(h):
                for t in range(NT):
                    u = NT * h + t
                    eng.wait_ge(att_s, u + 1)
                    if h:
                        eng.wait_ge(att_exp, u - 1)
                    src = PS[:, 4 + 2 * t:6 + 2 * t, :].rearrange("p b n -> p (b n)")[:, 0:768]
                    step(eng.copy_predicated(SCO[t], AM[:, t, :].bitcast(U32), src), att_masked)
                    step(eng.reduce_max(MX[:, u:u + 1], SCO[t], AX))
                    step(ts(MX[:, 8 + u:9 + u], MX[:, u:u + 1], -HD ** -0.5, None, ALU.mult), att_max)

            def softmax_out(h):
                for t in range(NT):
                    u = NT * h + t
                    eng.wait_ge(att_exp, u + 1)
                    step(eng.reciprocal(MX[:, 24 + u:25 + u], MX[:, 16 + u:17 + u]))
                    step(ts(PROB[t], PROB[t], MX[:, 24 + u:25 + u], None, ALU.mult), att_prob)

            def ya_copy(h):
                eng.wait_ge(att_o, h + 1)
                rows = slice(HD * (h % 2), HD * (h % 2) + HD)
                step(eng.tensor_copy(YAT[rows, h // 2, :], PS[rows, 6, 0:SEQ]), yat_ready)

            def branch_a(j):
                eng.wait_ge(a_done, j + 1)
                g = GA[:, 2 * j:2 * j + 2, :].rearrange("p c s -> p (c s)")
                step(tt(g, g, bank(j), ALU.mult), a_used)

            eng.wait_ge(qkat_ready, 6)
            for h in range(AH):
                softmax_in(h)
                softmax_out(h)
                if h >= 1:
                    branch_a(h - 1)
                ya_copy(h)
            branch_a(3)
            for j in range(4):
                eng.wait_ge(b_done, j + 1)
                ga, gb = (g[:, 2 * j:2 * j + 2, :].rearrange("p c s -> p (c s)") for g in (GA, GB))
                step(tt(gb, gb, bank(j), ALU.mult))
                step(tt(ga, ga, gb, ALU.add), m_ready)
            for n in range(4):
                t, c = n // 2, n % 2
                eng.wait_ge(mix_done, n + 1)
                xv = X[:, t, c * 512:c * 512 + 512]
                step(tt(xv, xv, bank(4 + n), ALU.add), x_mixed)
            turn_copy(2, HT, 8)
            eng.wait_ge(squares, 4)
            invert(SS[:, 2:2 + NT], D)
            eng.wait_ge(part_done, 1)
            step(eng.tensor_copy(LPART, bank(1, SEQ)), part_ready)
            step(eng.tensor_copy(RBB[:, :], bank(2, NE)))
            eng.wait_ge(log_done, 1)
            for t in range(NT):
                step(stt(out=LOG[:, t, :], in0=bank(3, NE, t * NE), scalar=SS[:, 2 + t:3 + t], in1=RBB[:, :], op0=ALU.mult, op1=ALU.add))
            for t in range(NT):
                step(eng.max(TOP[:, t, :], LOG[:, t, :]))
                step(eng.max_index(TOPI[:, t, :], TOP[:, t, :], LOG[:, t, :]))
            step(eng.tensor_copy(TOPF[:, :, :], TOPI[:, :, :]))
            step(ts(MX[:, 0:NT], TOP[:, :, 0], -1.0, None, ALU.mult), logits_max)
            four = [P, NT, TOPK, NE]
            hit = HITS.rearrange("p (t k e) -> p t k e", t=NT, k=TOPK)
            step(tt(hit, IO32[:, :].unsqueeze(1).unsqueeze(1).broadcast_to(four),
                    TOPF[:, :, 0:TOPK].unsqueeze(3).broadcast_to(four), ALU.is_equal))
            step(eng.reduce_sum(SEL[:, :, :], HITS.rearrange("p (t k e) -> p t e k", t=NT, k=TOPK), AX), sel_ready)
            eng.wait_ge(rank_done, 1)
            step(stt(out=RANKS[:, :, :].rearrange("p t e -> p (t e)"), in0=bank(5, NT * NE), scalar=1.0,
                     in1=SEL[:, :, :].rearrange("p t e -> p (t e)"), op0=ALU.add, op1=ALU.mult))

            def weights():
                eng.wait_ge(top_exp, 1)
                step(eng.reciprocal(MX[:, 4:4 + NT], MX[:, 2:2 + NT]))
                step(tt(TW[:, :, 0:TOPK], TW[:, :, 0:TOPK], MX[:, 4:4 + NT].unsqueeze(2).broadcast_to([P, NT, TOPK]), ALU.mult))
                step(tt(hit, hit, TW[:, :, 0:TOPK].unsqueeze(3).broadcast_to(four), ALU.mult))
                step(eng.reduce_sum(GATES[:, :, :], HITS.rearrange("p (t k e) -> p t e k", t=NT, k=TOPK), AX), gates_ready)
                eng.wait_ge(rank_done, 2)
                step(eng.reduce_max(CNT[:, :], bank(4, NE), AX))
                step(eng.tensor_copy(CNTI[:, :], CNT[:, :]), flag_ready)

            def choose(j):
                step1(tt(ONEHOT[:, :, :, :], IOS[:, :].unsqueeze(1).unsqueeze(1).broadcast_to([P, NT, 2, CAP]),
                         RANKS[:, :, bass.ds(2 * j, 2)].unsqueeze(3).broadcast_to([P, NT, 2, CAP]), ALU.is_equal))

            def step1(ins):
                ins.then_inc(onehot, 1)

            def weigh(j, n):
                eng.wait_ge(onehot, n)
                for e in range(2):
                    ins = tt(GD[:, e, :, :].rearrange("p t (u s) -> p t u s", u=2),
                             ONEHOT[:, :, e, :].unsqueeze(2).broadcast_to([P, NT, 2, CAP]),
                             GATES[:, :, bass.ds(2 * j + e, 1)].unsqueeze(3).broadcast_to([P, NT, 2, CAP]), ALU.mult)
                ins.then_inc(gd_ready, 1)

            def gathered(j, n):
                eng.wait_ge(ga_done, n)
                eng.tensor_copy(SELE[:, :, :], SELT[:, bass.ds(2 * j, 2)].unsqueeze(2).broadcast_to([P, 2, CAP])
                                ).then_inc(sele_ready, 1)
                tt(HTE, pair(2).rearrange("p (k s) -> p k s", k=KC),
                   COL[:, 8:16].unsqueeze(2).broadcast_to([P, KC, 2 * CAP]), ALU.mult).then_inc(ht_ready, 1)

            def swiglu(n):
                hid = pair(0).rearrange("p (f u) -> p f u", u=2)
                eng.wait_ge(hid_done, n)
                eng.tensor_scalar(GATE, hid[:, :, 0], LIMIT, None, ALU.min).then_inc(gate_in, 1)
                ts(UP, hid[:, :, 1], LIMIT, -LIMIT, ALU.min, ALU.max).then_inc(hid_read, 1)
                eng.wait_ge(hid_read, n)
                stt(out=UP, in0=UP, scalar=1.0, in1=GATE, op0=ALU.add, op1=ALU.mult).then_inc(glu_part, 1)
                eng.wait_ge(glu_part, n)
                eng.wait_ge(sig_ready, n)
                past(eng, at_done, n - 1)
                tt(A, UP, SIG, ALU.mult).then_inc(a_ready, 1)

            def add_x(n, t):
                eng.wait_ge(sc_done, 2 * n - 1 + t)
                tt(X[:, t, :], X[:, t, :], pair(6), ALU.add).then_inc(x_added, 1)

            def moe(q):
                first = q * PAIRS
                if not isinstance(q, int):
                    ts(IOS[:, :], IOS[:, :], float(CAP), None, ALU.add).then_inc(ios_moved, 1)
                    eng.wait_ge(ios_moved, q)
                    eng.wait_ge(tg_done, first)
                    eng.wait_ge(gd_ready, first)
                choose(0)
                if isinstance(q, int):
                    for t in range(NT):
                        step(ts(H[:, t, :], X[:, t, :], SS[:, 2 + t:3 + t], None, ALU.mult), h_ready)
                gathered(0, first + 1)
                if isinstance(q, int):
                    weights()
                    eng.wait_ge(gatt_done, 1)
                    step(eng.tensor_copy(GATT[:, :], PS[0:NE, 4, 0:SEQ]), gatt_ready)
                weigh(0, first + 1)

                def one(i, last):
                    m = first + i
                    if not last:
                        eng.wait_ge(ga_done, m + 1)
                        eng.wait_ge(gd_ready, m + 1)
                        choose(i + 1)
                    swiglu(2 * m + 1)
                    if not last:
                        eng.wait_ge(tg_done, m + 1)
                        weigh(i + 1, m + 2)
                    swiglu(2 * m + 2)
                    add_x(2 * m + 1, 0)
                    add_x(2 * m + 1, 1)
                    if not last:
                        gathered(i + 1, m + 2)
                    add_x(2 * m + 2, 0)
                    add_x(2 * m + 2, 1)

                one(0, False)
                with eng.Fori(1, PAIRS - 1) as i:
                    one(i, False)
                one(PAIRS - 1, True)

            runtime_pass(eng, moe)
            step(eng.memset(CNT[:, :], 0.0), x_final)
            turn_copy(3, HT, 16)
            eng.wait_ge(squares, 6)
            invert(SS[:, 12:12 + NT], D)
            eng.wait_ge(nf_in, 16)
            for t in range(NT):
                for c in range(2):
                    n = 2 * t + c
                    cols = slice(c * 512, c * 512 + 512)
                    eng.wait_ge(ple_sig, n + 1)
                    step(tt(H[:, t, cols], H[:, t, cols], PP[:, t, cols], ALU.mult))
                    step(tt(X[:, t, cols], X[:, t, cols], H[:, t, cols], ALU.add), x_final if c else dve_step)
                eng.wait_ge(squares, 7 + t)
                invert(SS[:, 14 + t:15 + t], D)
                step(stt(out=X[:, t, :], in0=X[:, t, :], scalar=SS[:, 14 + t:15 + t], in1=NF, op0=ALU.mult, op1=ALU.mult), fin_ready)

        @block.tensor
        def _(eng):
            mm = eng.matmul
            eng.wait_ge(iotas, 1)
            eng.wait_ge(vec_in, 80)
            eng.transpose(bank(7, 40), VEC[:, :], IDENT[0:40, 0:40]).then_inc(vec_turned, 1)

            def turn(use, src):
                for j in range(4):
                    for c in range(2):
                        for t in range(NT):
                            f = (2 * j + c) * P
                            ins = eng.transpose(bank(4 + j, P, c * SEQ + t * P), src[:, t, f:f + P], IDENT[:, :])
                    ins.then_inc(turned, 1)

            eng.wait_ge(h_ready, 2)
            eng.wait_ge(cols_ready, 1)
            turn(0, H)

            def slab(i):
                c0, w, by_feature = SLABS[i]
                eng.wait_ge(slab_in[i % 2], 16 * (i // 2 + 1))
                if i >= 2:
                    mine, n = emptied(i - 2)
                    eng.wait_ge(slab_dve if mine else slab_act, n)
                wv = SLAB[i % 2]
                if by_feature:
                    for c in range(-(-w // P)):
                        m = min(P, w - c * P)
                        for k in range(KC):
                            ins = mm(PS[0:m, 2 * (i % 2) + c // 2, c % 2 * SEQ:c % 2 * SEQ + SEQ], wv[:, k, c * P:c * P + m],
                                     HT[:, k, :], start=k == 0, stop=k == KC - 1)
                else:
                    for t in range(NT):
                        for k in range(KC):
                            ins = mm(bank(2 * (i % 2) + t, w), HT[:, k, t * P:(t + 1) * P], wv[:, k, 0:w],
                                     start=k == 0, stop=k == KC - 1)
                ins.then_inc(slab_done, 1)

            eng.wait_ge(turn_read, 4)
            for i in range(3):
                slab(i)
            eng.wait_ge(u_in, 32)
            eng.wait_ge(slab_dve, 1)
            for c in range(8):
                ins = mm(bank(4 + c // 2, SEQ, c % 2 * SEQ), UB[:, c * P:(c + 1) * P], LOWT[:, :], start=True, stop=True)
            ins.then_inc(z_done, 1)
            for i in range(3, 9):
                slab(i)
            eng.wait_ge(qt_ready, 1)
            eng.wait_ge(z_read, 1)
            for d in range(2):
                for h in range(GH):
                    for c in range(NCH):
                        f = (d * GH + h) * SEQ + c * CH
                        rows = slice(c % 2 * CH, c % 2 * CH + CH)
                        ins = mm(PS[rows, 4 + d, h * P + c // 2 * CH:h * P + c // 2 * CH + CH], KT_[:, f:f + CH],
                                 QT_[:, f:f + CH], start=True, stop=True)
            ins.then_inc(scores_done, 1)
            eng.wait_ge(kst_ready, 1)
            for n in range(4):
                t, d = n // 2, n % 2
                if n >= 2:
                    eng.wait_ge(kstok_ready, n - 1)
                for h in range(GH):
                    f = (d * GH + h) * SEQ + t * P
                    ins = eng.transpose(bank(6 + n % 2, DK, h * DK), KST[:, f:f + P], IDENT[:, :])
                ins.then_inc(kst_turned, 1)
            slab(9)
            eng.wait_ge(slab_dve, 3)
            eng.wait_ge(st_ready, 2)
            eng.wait_ge(kstok_ready, 4)
            for s in range(NCH - 1):
                for dh in range(DH):
                    d, h = dh // GH, dh % GH
                    c = s if d == 0 else NCH - 1 - s
                    rows = slice(c % 2 * CH, c % 2 * CH + CH)
                    if s:
                        eng.wait_ge(state_ready, 8 * (s - 1) + 2 * (dh // 2) + 2)
                    ins = mm(bank(4 + dh // 2, DV, dh % 2 * DV), KSTOK[rows, c // 2, dh * DK:(dh + 1) * DK],
                             V[rows, c // 2, h * DV:(h + 1) * DV], start=True, stop=True)
                    if dh % 2:
                        ins.then_inc(kv_done, 1)
            slab(10)
            eng.wait_ge(state_ready, 8 * (NCH - 1))
            for c in range(NCH):
                t, rows = c // 2, slice(c % 2 * CH, c % 2 * CH + CH)
                for h in range(GH):
                    o = PS[rows, 4 + 2 * t + h // 2, h % 2 * DV:h % 2 * DV + DV]
                    parts = [(ST[rows, h * P + t * CH:h * P + t * CH + CH], V[rows, t, h * DV:(h + 1) * DV])]
                    if c > 0:
                        parts.append((QIN[:, h * SEQ + c * CH:h * SEQ + c * CH + CH], STATE[8 * (c - 1) + h]))
                    if c < NCH - 1:
                        f = (GH + h) * SEQ + c * CH
                        parts.append((QIN[:, f:f + CH], STATE[8 * (NCH - 2 - c) + GH + h]))
                    for n, (l, r) in enumerate(parts):
                        ins = mm(o, l, r, start=n == 0, stop=n == len(parts) - 1)
            ins.then_inc(o_done, 1)
            slab(11)
            slab(12)
            eng.wait_ge(y_ready, 8)
            turn(1, R)
            eng.wait_ge(rotated, 2)
            eng.wait_ge(turn_read, 8)
            for n in range(6):
                if n >= 4:
                    eng.wait_ge(qkat_ready, n - 3)
                for c in range(2):
                    for t in range(NT):
                        f = (2 * n + c) * P
                        ins = eng.transpose(bank(4 + n % 4, P, c * SEQ + t * P), QKA[:, t, f:f + P], IDENT[:, :])
                ins.then_inc(qka_turned, 1)

            def scores(h):
                rows = slice(HD * (h % 2), HD * (h % 2) + HD)
                if h == 0:
                    eng.wait_ge(qkat_ready, 6)
                else:
                    eng.wait_ge(pt_ready, NT * h)
                    eng.wait_ge(yat_ready, h)
                for t in range(NT):
                    for g in range(GROUPS):
                        c = (g * AH + h) // 2
                        ins = mm(PS[:, 4 + 2 * t + g // 2, g % 2 * SEQ:g % 2 * SEQ + SEQ], QKAT[rows, c, t * P:(t + 1) * P],
                                 QKAT[rows, 6 + c, :], start=True, stop=True)
                    ins.then_inc(att_s, 1)

            def probs(h):
                for t in range(NT):
                    eng.wait_ge(att_prob, NT * h + t + 1)
                    for c in range(6):
                        ins = eng.transpose(PS[:, 4 + 2 * t + c // 4, c % 4 * P:c % 4 * P + P], PROB[t][:, c * P:(c + 1) * P],
                                            IDENT[:, :])
                    ins.then_inc(att_t, 1)

            def head_out(h):
                eng.wait_ge(pt_ready, NT * h + NT)
                if h == 0:
                    eng.wait_ge(slab_dve, 5)
                rows = slice(HD * (h % 2), HD * (h % 2) + HD)
                for c in range(6):
                    head, jt = c // 2 * AH + h, c % 2
                    ins = mm(PS[rows, 6, 0:SEQ], VA[:, jt, head * HD:(head + 1) * HD], PT[:, c, :], start=c == 0, stop=c == 5)
                ins.then_inc(att_o, 1)

            def branch(j, wv, src, nk, done):
                for c in (2 * j, 2 * j + 1):
                    for k in range(nk):
                        ins = mm(bank(j, SEQ, c % 2 * SEQ), wv[:, k, c * P:(c + 1) * P], src[:, k, :], start=k == 0, stop=k == nk - 1)
                ins.then_inc(done, 1)

            def branch_a(j):
                if j % 2 == 0:
                    eng.wait_ge(slab_act, emptied(14 + j // 2)[1])
                if j == 0:
                    eng.wait_ge(wa_in, 16)
                branch(j, W_A, YT, KC, a_done)

            scores(0)
            slab(13)
            probs(0)
            slab(14)
            head_out(0)
            scores(1)
            slab(15)
            probs(1)
            branch_a(0)
            head_out(1)
            scores(2)
            branch_a(1)
            probs(2)
            branch_a(2)
            head_out(2)
            scores(3)
            branch_a(3)
            probs(3)
            head_out(3)
            eng.wait_ge(yat_ready, AH)
            eng.wait_ge(wb_in, 16)
            for j in range(4):
                eng.wait_ge(a_used, j + 1)
                branch(j, W_B, YAT, 2, b_done)
            eng.wait_ge(p_in, 32)
            eng.wait_ge(m_ready, 4)
            for c in range(2):
                for t in range(NT):
                    ins = eng.transpose(bank(0, P, c * SEQ + t * P), PTOK[:, t, c * P:(c + 1) * P], IDENT[:, :])
            ins.then_inc(p_turned, 1)
            eng.wait_ge(wout_in, 16)
            for n in range(4):
                t, c = n // 2, n % 2
                for k in range(KC):
                    ins = mm(bank(4 + n), GA[:, k, t * P:(t + 1) * P], W_OUT[:, k, c * 512:c * 512 + 512], start=k == 0, stop=k == KC - 1)
                ins.then_inc(mix_done, 1)
            eng.wait_ge(small_in, 32)
            mm(bank(2, NE), ONES[0:1, :], RB[:, :], start=True, stop=True)
            eng.wait_ge(x_mixed, 4)
            turn(2, X)
            for i in range(2):
                for g in range(4):
                    k = 2 * g + i
                    eng.wait_ge(turn_read, 9 + g)
                    ins = mm(PS[NE * g:NE * g + NE, 1, 0:SEQ], RW[:, k, :], HT[:, k, :], start=i == 0, stop=i == 1)
            ins.then_inc(part_done, 1)
            eng.wait_ge(part_ready, 1)
            for t in range(NT):
                ins = mm(bank(3, NE, t * NE), LPART[:, t * P:(t + 1) * P], SEL4[:, :], start=True, stop=True)
            ins.then_inc(log_done, 1)

            def embed(t):
                for c in range(2):
                    for k in range(2):
                        ins = mm(bank(6 * t + c), PTT[:, k, t * P:(t + 1) * P], W_P[:, k, c * 512:c * 512 + 512], start=k == 0, stop=k == 1)
                ins.then_inc(pp_done, 1)

            eng.wait_ge(ptt_ready, 1)
            embed(0)
            eng.wait_ge(sel_ready, 1)
            mm(bank(5, NT * NE), TRI[:, :], SEL[:, :, :].rearrange("p t e -> p (t e)"), start=True, stop=False)
            mm(bank(5, NE, NE), ONES[:, :], SEL[:, 0, :], start=False, stop=True).then_inc(rank_done, 1)
            for t in range(NT):
                ins = mm(bank(4, NE), ONES[:, :], SEL[:, t, :], start=t == 0, stop=t == NT - 1)
            ins.then_inc(rank_done, 1)

            def gather(n):
                eng.wait_ge(onehot, n)
                past(eng, ht_ready, n - 1)
                for k in range(KC):
                    for t in range(NT):
                        ins = mm(PS[:, 2 + k // 4, k % 4 * P:k % 4 * P + P], H[:, t, k * P:(k + 1) * P],
                                 ONEHOT[:, t, :, :].rearrange("p e s -> p (e s)"), start=t == 0, stop=t == NT - 1)
                ins.then_inc(ga_done, 1)

            def hidden(n, e):
                past(eng, hid_read, n - 1)
                for c in range(4):
                    h = CAP * (c // 2)
                    mm(PS[h:h + CAP, c % 2, :], SELE[:, e, :], B1P[:, c * 512:c * 512 + 512], start=True, stop=False)
                for k in range(KC):
                    eng.wait_ge(land[k], n * 16)
                    for c in (0, 2, 1, 3):
                        h = CAP * (c // 2)
                        ins = mm(PS[h:h + CAP, c % 2, :], HTE[:, k, e * CAP:(e + 1) * CAP], RING[:, k, c * 512:c * 512 + 512],
                                 start=False, stop=k == KC - 1)
                    if k < KC - 1:
                        ins.then_inc(w_used, 1)
                ins.then_inc(hid_done, 1)

            def down(n):
                eng.wait_ge(at_ready, n)
                for f in range(KC):
                    if f % 2 == 0:
                        eng.wait_ge(land[8 + f // 2], n * 16)
                    for h in range(2):
                        ins = mm(PS[CAP * h:CAP * h + CAP, 4, :], AT[:, f % 4 * P + f // 4 * CAP:f % 4 * P + f // 4 * CAP + CAP],
                                 RING[:, 8 + f // 2, f % 2 * D + h * 512:f % 2 * D + h * 512 + 512], start=f == 0, stop=f == KC - 1)
                    if f % 2 and f < KC - 1:
                        ins.then_inc(w_used, 1)
                ins.then_inc(oe_done, 1)

            def turn_a(n):
                eng.wait_ge(a_ready, n)
                past(eng, at_ready, n - 1)
                for c in range(4):
                    ins = eng.transpose(bank(5, P, c * P), A[:, c * P:(c + 1) * P], IDENT[:, :])
                ins.then_inc(at_done, 1)

            def scatter(n, e, t):
                eng.wait_ge(oe_ready, n)
                past(eng, x_added, 2 * n - 2 + t)
                first = isinstance(n, int) and n == 1
                for h in range(2):
                    if first:
                        if h == 0:
                            eng.wait_ge(b2_in, 16)
                        mm(bank(6 + h), GATT[:, t * P:(t + 1) * P], UB[:, h * 512:h * 512 + 512], start=True, stop=False)
                for h in range(2):
                    ins = mm(bank(6 + h), GT[CAP * h:CAP * h + CAP, e, t, :], OUTE[CAP * h:CAP * h + CAP, :], start=not first, stop=True)
                ins.then_inc(sc_done, 1)

            def moe(q):
                first = q * PAIRS
                if isinstance(q, int):
                    eng.wait_ge(h_ready, 4)
                gather(first + 1)
                if isinstance(q, int):
                    embed(1)
                    eng.wait_ge(gates_ready, 1)
                    eng.wait_ge(flag_ready, 1)
                    for t in range(NT):
                        ins = eng.transpose(PS[0:NE, 4, t * P:(t + 1) * P], GATES[:, t, :], IDENT[:, :])
                    ins.then_inc(gatt_done, 1)
                    eng.wait_ge(b1p_ready, 3)
                    eng.wait_ge(pp_ready, 2)

                def one(i, last):
                    m = first + i
                    n = 2 * m
                    eng.wait_ge(ht_ready, m + 1)
                    hidden(n + 1, 0)
                    eng.wait_ge(gd_ready, m + 1)
                    past(eng, oe_ready, n)
                    if isinstance(m, int):
                        eng.wait_ge(gatt_ready, 1)
                    for e in range(2):
                        for t in range(NT):
                            ins = eng.transpose(bank(4, P, (2 * e + t) * P), GD[:, e, t, :], IDENT[:, :])
                    ins.then_inc(tg_done, 1)
                    if not last:
                        gather(m + 2)
                    turn_a(n + 1)
                    eng.wait_ge(gt_ready, m + 1)
                    down(n + 1)
                    hidden(n + 2, 1)
                    scatter(n + 1, 0, 0)
                    turn_a(n + 2)
                    scatter(n + 1, 0, 1)
                    eng.wait_ge(oe_ready, n + 1)
                    down(n + 2)
                    scatter(n + 2, 1, 0)
                    scatter(n + 2, 1, 1)

                one(0, False)
                with eng.Fori(1, PAIRS - 1) as i:
                    one(i, False)
                one(PAIRS - 1, True)

            runtime_pass(eng, moe)
            eng.wait_ge(x_final, 1)
            turn(3, X)
            eng.wait_ge(turn_read, 16)
            eng.wait_ge(wg_in, 16)
            for n in range(4):
                t, c = n // 2, n % 2
                for k in range(KC):
                    ins = mm(bank(n), HT[:, k, t * P:(t + 1) * P], W_G[:, k, c * 512:c * 512 + 512], start=k == 0, stop=k == KC - 1)
                ins.then_inc(pleg_done, 1)


_INS = ["x", "p", "positions", "norm_mix", "w_in", "gla_fgate_up", "gla_fgate_bias", "gla_out_norm", "w_branch_gla",
        "w_branch_attn", "w_out", "norm_ffn", "router_w", "router_b", "expert_w1", "expert_b1", "expert_w2", "expert_b2",
        "norm_ple", "ple_gate_w", "ple_proj", "norm_final"]


def kernel(**inputs):
    import numpy as _np
    import concourse.bacc as _bacc
    from concourse import mybir as _mybir
    from concourse.bass_utils import run_bass_kernel_spmd as _run

    nc = _bacc.Bacc("TRN2", target_bir_lowering=False, num_devices=1)
    arrays, args = {}, []
    for name in _INS:
        a = _np.ascontiguousarray(inputs[name])
        arrays[f"in_{name}"] = a
        args.append(nc.dram_tensor(f"in_{name}", a.shape, _mybir.dt.from_np(a.dtype), kind="ExternalInput").ap())
    args.append(nc.dram_tensor("out_0", (1, SEQ, D), _mybir.dt.float32, kind="ExternalOutput").ap())
    build(nc, *args)
    r = _run(nc, [arrays], core_ids=[0])
    return r.results[0]["out_0"]
```

```python
from contextlib import ExitStack
import math

import numpy as np
import concourse.bass as bass
from concourse import mybir

F32 = mybir.dt.float32
BF16 = mybir.dt.bfloat16
I32 = mybir.dt.int32
U32 = mybir.dt.uint32
ALU = mybir.AluOpType
ACT = mybir.ActivationFunctionType
AX = mybir.AxisListType.X

P = 128
D = 1024
SEQ = 256
NT = SEQ // P
KC = D // P
EPS = 1e-6
BANK = 512

GH, DK, DV = 4, 128, 256
RANK = 16
TAU = 16.0
CH = 64
NCH = SEQ // CH
AH, HD, GROUPS = 4, 64, 3
AHEADS = AH * GROUPS
AW = AHEADS * HD
ROT = HD // 4
HALF = ROT // 2
THETA = 500000.0
NEG = -1e30
PLE = 256
NE, TOPK = 32, 4
CAP = 64
PAIRS = NE // 2
PASSES = SEQ // CAP
ALPHA, LIMIT = 1.702, 7.0
WSLOTS1, WSLOTS2 = 8, 4
WSLOTS = WSLOTS1 + WSLOTS2
TWICE = 2
USES = WSLOTS - 2

C_Q, C_K = 0, GH * DK
C_V = C_K + GH * DK
C_R = C_V + GH * DV
C_LOW = C_R + GH * DV
C_QA = C_LOW + 2 * RANK
C_VA = C_QA + 2 * AW
C_GA = C_VA + AW
C_GB = C_GA + D
SLABS = [(C_LOW, 2 * RANK, True), (C_Q, 512, True), (C_K, 512, True), (C_V, 512, False), (C_V + 512, 512, False),
         (C_QA, 512, False), (C_QA + 512, 512, False), (C_QA + 1024, 512, False),
         (C_VA, 512, False), (C_VA + 512, AW - 512, False), (C_R, 512, False), (C_R + 512, 512, False),
         (C_GA, 512, True), (C_GA + 512, 512, True), (C_GB, 512, True), (C_GB + 512, 512, True)]
DVE_SLABS = (0, 3, 4, 8, 9, 10, 11)


def emptied(i):
    mine = i in DVE_SLABS
    return mine, sum((j in DVE_SLABS) == mine for j in range(i + 1))


def build(nc, x, p, positions, norm_mix, w_in, fgate_up, fgate_bias, out_norm, w_gla, w_att, w_out, norm_ffn,
          router_w, router_b, w1, b1, w2, b2, norm_ple, ple_gate_w, ple_proj, norm_final, out):
    with ExitStack() as ctx:
        def sb(name, shape, dt=F32):
            return ctx.enter_context(nc.sbuf_tensor(name, shape, dt))

        def sem(name):
            return ctx.enter_context(nc.semaphore(name))

        RING = sb("RING", [P, WSLOTS, 2048])
        ringf = RING[:, :, :].rearrange("p s n -> p (s n)")
        AREA = sb("AREA", [P, 96 * 256])

        def at(kib, n):
            return AREA[:, kib * 256:kib * 256 + n]

        def slot(i, n, base=0):
            return ringf[:, i * 2048 + base:i * 2048 + base + n]

        SLAB = [slot(8 + 2 * b, 4096).rearrange("p (k n) -> p k n", k=KC) for b in range(2)]
        W_OUT = slot(8, KC * D).rearrange("p (k n) -> p k n", k=KC)
        W_A = slot(0, KC * D).rearrange("p (k n) -> p k n", k=KC)
        DH = 2 * GH
        G_B0 = slot(0, 2048)
        G_B1 = slot(1, 2048)
        QT_ = slot(2, 2048)
        KT_ = slot(3, 2048)
        QIN = slot(4, 2048)
        KST = slot(5, 2048)
        G_E = slot(6, 2048)
        G_D = slot(7, 2048)
        RESET = slot(4, DH // 2 * SEQ)
        IOT = slot(5, 2 * 256).bitcast(I32).rearrange("p (t j) -> p t j", t=2)
        IOT2 = slot(5, 2 * 256, 512).bitcast(I32).rearrange("p (t j) -> p t j", t=2)
        KSTOK = G_E.rearrange("p (t f) -> p t f", t=NT)
        b3 = lambda v: v.rearrange("p (f s) -> p f s", s=SEQ)
        STATE = [G_D[:, i * DV:(i + 1) * DV] for i in range(8)] + [G_B0[:, i * DV:(i + 1) * DV] for i in range(8)] \
            + [G_B1[:, i * DV:(i + 1) * DV] for i in range(8)]
        QKAT = slot(4, 12 * SEQ).rearrange("p (c s) -> p c s", s=SEQ)
        SCO = [slot(4, 768, 3072), slot(4, 768, 3840)]
        PROB = [slot(4, 768, 4608), slot(4, 768, 5376)]
        PT = slot(4, 6 * SEQ, 6144).rearrange("p (c s) -> p c s", s=SEQ)

        YAT = slot(4, 2 * SEQ, 7680).rearrange("p (c s) -> p c s", s=SEQ)

        X = at(0, 2048).rearrange("p (t d) -> p t d", t=NT)
        H = at(8, 2048).rearrange("p (t d) -> p t d", t=NT)
        HT = at(16, 2048).rearrange("p (k s) -> p k s", k=KC)
        QK_T = at(24, 2048)
        YT = at(24, 2048).rearrange("p (k s) -> p k s", k=KC)
        V = at(32, 2048).rearrange("p (t d) -> p t d", t=NT)
        R = at(40, 2048).rearrange("p (t d) -> p t d", t=NT)
        GA = at(48, 2048).rearrange("p (k s) -> p k s", k=KC)
        GB = at(56, 2048).rearrange("p (k s) -> p k s", k=KC)
        QKA = at(64, 3072).rearrange("p (t f) -> p t f", t=NT)
        VA = at(76, 1536).rearrange("p (t f) -> p t f", t=NT)
        AM = at(82, 1536).bitcast(I32).rearrange("p (t j) -> p t j", t=NT)
        W_B = at(88, 2048).rearrange("p (k n) -> p k n", k=2)
        ROTB = [at(8 + 2 * i, 384).rearrange("p (t h j) -> p t h j", t=NT, j=HALF) for i in range(4)]
        JUNK = at(16, 2048)
        YJUNK = at(8, 2048)
        W1 = [[slot(k, 2048) for k in range(WSLOTS1)], [at(16, 2048), at(24, 2048)] + [slot(k, 2048) for k in range(2, WSLOTS1)]]
        W2 = [[at(32 + 8 * f, 2048) for f in range(WSLOTS2)], [slot(WSLOTS1 + f, 2048) for f in range(WSLOTS2)]]
        W_G = at(32, KC * D).rearrange("p (k n) -> p k n", k=KC)
        B1S = at(40, 2048)
        B1P = at(64, 1024).bitcast(BF16)
        HTE = at(68, 1024).rearrange("p (k s) -> p k s", k=KC)
        GT = at(72, 512).rearrange("p (e t s) -> p e t s", e=2, t=NT)
        GD = at(74, 512).rearrange("p (e t f) -> p e t f", e=2, t=NT)
        GATE, SIG, UP = at(76, 512), at(78, 512), at(80, 512)
        HITS = at(76, NT * TOPK * NE)
        A, AT, OUTE = at(82, 512), at(84, 512), at(86, 512)
        PTOK = at(84, 512).rearrange("p (t d) -> p t d", t=NT)
        PTT = at(86, 512).rearrange("p (k s) -> p k s", k=2)
        PP = at(88, 2048).rearrange("p (t d) -> p t d", t=NT)
        W_P = at(24, 2048).rearrange("p (k n) -> p k n", k=2)
        NF = at(76, 1024)
        LPART = at(82, SEQ)
        ONEHOT = sb("ONEHOT", [P, NT, 2, CAP])

        IDENT = sb("IDENT", [P, P])
        ONES = sb("ONES", [P, P])
        TRI = sb("TRI", [P, P])
        MF = sb("MF", [P, CH])
        MB = sb("MB", [P, CH])
        IOS = sb("IOS", [P, CAP])
        IO32 = sb("IO32", [P, NE])
        UB = sb("UB", [NE, D])
        VEC = slot(6, P)[0:40, :]
        COL = sb("COL", [P, 40])
        RW = sb("RW", [P, KC, NE])
        RB = sb("RB", [1, NE])
        RBB = sb("RBB", [P, NE])
        SEL4 = sb("SEL4", [P, NE])
        LOWT = sb("LOWT", [2 * RANK, SEQ])
        DEC = sb("DEC", [P, DH * NCH])
        ST = sb("ST", [P, 512])
        SS = sb("SS", [P, 16])
        POSI = sb("POSI", [P, NT], I32)
        POSF = sb("POSF", [P, NT])
        INVF = sb("INVF", [P, HALF])
        ANG = sb("ANG", [P, 2, NT * HALF])
        TRN = sb("TRN", [P, 2, NT * HALF])
        TURN_I = sb("TURN_I", [P, 2, NT * HALF], I32)
        CS = sb("CS", [P, 2, NT * HALF])
        MX = sb("MX", [P, 4 * 8])
        LOG = sb("LOG", [P, NT, NE])
        TOP = sb("TOP", [P, NT, 8])
        TOPI = sb("TOPI", [P, NT, 8], U32)
        TOPF = sb("TOPF", [P, NT, 8])
        TW = sb("TW", [P, NT, 8])
        GATES = sb("GATES", [P, NT, NE])
        SEL = sb("SEL", [P, NT, NE])
        RANKS = sb("RANKS", [P, NT, NE])
        GATT = sb("GATT", [NE, SEQ])
        CNT = sb("CNT", [P, 1])
        CNTI = sb("CNTI", [P, 1], I32)
        SELT = sb("SELT", [P, NE], BF16)
        SELE = sb("SELE", [P, 2, CAP], BF16)
        SELI = sb("SELI", [P, 2, NE], I32)

        PS = ctx.enter_context(nc.psum_tensor("PS", [P, 8, BANK], F32))

        def bank(i, n=BANK, base=0):
            return PS[:, i, base:base + n]

        def pair(i):
            return PS[:, i:i + 2, :].rearrange("p b n -> p (b n)")

        dve_step, act_step, pool_step = sem("dve_step"), sem("act_step"), sem("pool_step")
        x_in = [sem("x_in0"), sem("x_in1")]
        vec_in, small_in, pos_in = sem("vec_in"), sem("small_in"), sem("pos_in")
        slab_in = [sem("slab_in0"), sem("slab_in1")]
        wa_in, wb_in, wout_in, p_in, b1_in, b2_in = (sem(n) for n in ("wa_in", "wb_in", "wout_in", "p_in", "b1_in", "b2_in"))
        wg_in, nf_in, u_in, out_written = [sem("wg_in0"), sem("wg_in1")], sem("nf_in"), sem("u_in"), sem("out_written")
        u_zero, ones_set, iotas = sem("u_zero"), sem("ones_set"), sem("iotas")
        squares, h_ready, turned, turn_read = sem("squares"), sem("h_ready"), sem("turned"), sem("turn_read")
        inv_ready, rms_ready = sem("inverse_ready"), sem("rms_ready")
        vec_turned, cols_ready = sem("vec_turned"), sem("cols_ready")
        slab_done, slab_act, slab_dve, sil = sem("slab_done"), sem("slab_emptied_act"), sem("slab_emptied_dve"), sem("r_sigmoid")
        z_done, z_read, lse_part, g_cum = sem("z_done"), sem("z_read"), sem("z_log"), sem("g_cum")
        diff, expd, expd_used = sem("gla_diff"), sem("gla_exp"), sem("gla_exp_used")
        qt_ready, kst_ready, scores_done, st_ready = sem("qt_ready"), sem("kst_ready"), sem("gla_scores"), sem("st_ready")
        kst_turned, kstok_ready, kv_done, state_ready = sem("kst_turned"), sem("kstok_ready"), sem("kv_done"), sem("state_ready")
        o_done, o_sq, y_ready = sem("o_done"), sem("o_squares"), sem("y_ready")
        ang_ready, trig, rotated = sem("ang_ready"), sem("trig_ready"), sem("rotated")
        qka_turned, qkat_ready = sem("qka_turned"), sem("qkat_ready")
        att_s, att_masked, att_max, att_exp, att_prob = (sem(n) for n in ("att_scores", "att_masked", "att_max", "att_exp", "att_prob"))
        att_t, pt_ready, att_o, yat_ready = sem("att_turned"), sem("pt_ready"), sem("att_out"), sem("yat_ready")
        a_done, a_used, b_done, m_ready = sem("branch_a_done"), sem("branch_a_used"), sem("branch_b_done"), sem("merged")
        mix_done, x_mixed = sem("mix_done"), sem("x_mixed")
        p_turned, ptt_ready, pp_done, pp_ready = sem("p_turned"), sem("ptt_ready"), sem("pp_done"), sem("pp_ready")
        log_done, logits_max, top_exp = sem("log_done"), sem("top_ready"), sem("top_exp")
        sel_ready, rank_done, gatt_done, gatt_ready = (sem(n) for n in ("sel_ready", "rank_done", "gatt_done", "gatt_ready"))
        flag_ready, b1p_ready, bias_done = sem("flag_ready"), sem("b1p_ready"), sem("bias_done")
        land1 = [[sem(f"w1_land{s}") for s in range(WSLOTS1)]]
        land1.append([sem(f"w1_land{s}_1") for s in range(TWICE)] + land1[0][TWICE:])
        land2 = [[sem(f"w2_land{e}_{s}") for s in range(WSLOTS2)] for e in range(2)]
        w_used = sem("w_used")
        onehot, gd_ready, tg_done, gt_ready = sem("onehot_ready"), sem("gd_ready"), sem("gd_turned"), sem("gt_ready")
        ga_done, ht_ready, hid_done, gate_in = sem("gathered"), sem("hte_ready"), sem("hid_done"), sem("gate_ready")
        hid_read, glu_part, sig_ready, a_ready = sem("hid_read"), sem("glu_part"), sem("sig_ready"), sem("a_ready")
        at_done, at_ready, oe_done, oe_ready = sem("a_turned"), sem("at_ready"), sem("expert_out"), sem("oute_ready")
        sc_done, x_added, pleg_done, ple_sig = sem("scattered"), sem("x_added"), sem("ple_gate_done"), sem("ple_sig")
        part_done, part_ready, gates_ready, fin_ready, x_final, sele_ready, ios_moved = sem("part_done"), sem("part_ready"), sem("gates_ready"), sem("fin_ready"), sem("x_final"), sem("sele_ready"), sem("ios_moved")

        def steps(eng, own):
            count = {}

            def step(ins, s=own):
                count[s.name] = count.get(s.name, 0) + 1
                ins.then_inc(s, 1)
                eng.wait_ge(s, count[s.name])
            return step

        def past(eng, s, n):
            if not isinstance(n, int) or n > 0:
                eng.wait_ge(s, n)

        def runtime_pass(eng, body):
            body(0)
            eng.wait_ge(flag_ready, 1)
            most = eng.value_load(CNTI[0:1, 0:1], min_val=0, max_val=SEQ)
            with eng.If(most > CAP):
                with eng.Fori(1, PASSES) as q:
                    body(q)
            eng.nop()

        block = ctx.enter_context(nc.Block())

        @block.sync
        def _(eng):
            for t in range(NT):
                eng.dma_start(X[:, t, :], x[0, t * P:(t + 1) * P, :]).then_inc(x_in[t], 16)

            def load_slab(i):
                c0, w, _ = SLABS[i]
                if i == 1:
                    eng.wait_ge(vec_in, 80)
                if i >= 2:
                    eng.wait_ge(slab_done, i - 1)
                eng.dma_start(SLAB[i % 2][:, :, 0:w], w_in[0, :, c0:c0 + w].rearrange("(k p) n -> p k n", p=P)
                              ).then_inc(slab_in[i % 2], 16)

            def load_w1(e, half, n, slots):
                for k in slots:
                    before = n - (2 if k < TWICE else 1)
                    if not isinstance(n, int) or before >= 0:
                        if k == WSLOTS1 - 1:
                            eng.wait_ge(hid_done, before + 1)
                        else:
                            eng.wait_ge(w_used, before * USES + k + 1)
                    eng.dma_start(W1[half][k], w1[0, e, k * P:(k + 1) * P, :]).then_inc(land1[half][k], 16)

            def load_w2(e, half, n, slots):
                for f in slots:
                    if f == WSLOTS2 - 1:
                        past(eng, oe_done, n - 1)
                    elif not isinstance(n, int) or n > 0:
                        eng.wait_ge(w_used, (n - 2) * USES + WSLOTS1 + f)
                    eng.dma_start(W2[half][f].rearrange("p (a n) -> p a n", a=2),
                                  w2[0, e, f * 2 * P:(f + 1) * 2 * P, :].rearrange("(a p) n -> p a n", p=P)
                                  ).then_inc(land2[half][f], 16)

            for i in range(12):
                load_slab(i)
            eng.dma_start(W_B, w_att[0].rearrange("(k p) n -> p k n", p=P)).then_inc(wb_in, 16)
            eng.wait_ge(z_done, 1)
            eng.dma_start(UB[:, :], b2[0]).then_inc(b2_in, 16)
            load_slab(12)
            load_slab(13)
            eng.wait_ge(y_ready, 8)
            eng.dma_start(W_A, w_gla[0].rearrange("(k p) n -> p k n", p=P)).then_inc(wa_in, 16)
            load_slab(14)
            eng.wait_ge(turned, 8)
            for r in range(3):
                eng.dma_start(B1S[32 * r:32 * r + 32, :], b1[0]).then_inc(b1_in, 16)
            load_slab(15)
            eng.wait_ge(slab_done, len(SLABS))
            eng.dma_start(W_OUT, w_out[0].rearrange("(k p) n -> p k n", p=P)).then_inc(wout_in, 16)
            eng.wait_ge(a_done, 4)
            eng.dma_start(W_P, ple_proj[0].rearrange("(k p) n -> p k n", p=P)).then_inc(p_in, 16)
            eng.wait_ge(att_masked, AH * NT)
            eng.dma_start(PTOK, p[0, 0].rearrange("(t p) d -> p t d", p=P)).then_inc(p_in, 16)
            load_w1(0, 0, 0, range(4))
            eng.wait_ge(b_done, 4)
            load_w1(0, 0, 0, range(4, 8))
            eng.wait_ge(b1p_ready, 3)
            eng.wait_ge(m_ready, 4)
            load_w2(0, 0, 0, (0, 1, 3))
            eng.wait_ge(mix_done, 4)
            load_w2(0, 0, 0, (2,))
            load_w2(1, 1, 0, range(4))

            def experts(q):
                if isinstance(q, int):
                    eng.wait_ge(part_done, 1)
                    load_w1(1, 1, 1, [0])
                    load_w1(1, 1, 1, range(2, 6))
                    eng.wait_ge(pp_done, 2)
                    load_w1(1, 1, 1, (1, 6, 7))
                with eng.Fori(2 if isinstance(q, int) else 0, NE - 1, 2) as first:
                    if not isinstance(q, int):
                        eng.wait_ge(wg_in[0], q * 16)
                        eng.wait_ge(wg_in[1], q * 16)
                    for e in range(2):
                        n = q * NE + first + e
                        load_w1(first + e, e, n, range(8))
                        load_w2(first + e, e, n, range(4))
                eng.wait_ge(oe_done, q * NE + NE - 1)
                for i, k in enumerate((0, KC // 2)):
                    eng.dma_start(W_G[:, k:k + KC // 2, :], ple_gate_w[0, k * P:(k + KC // 2) * P, :].rearrange(
                        "(k p) n -> p k n", p=P)).then_inc(wg_in[i], 16)

            runtime_pass(eng, experts)
            eng.wait_ge(x_final, 1)
            eng.dma_start(NF, norm_final.rearrange("(a n) -> a n", a=1).to_broadcast([P, D])).then_inc(nf_in, 16)
            for n in range(2 * NT):
                t, cols = n // 2, slice(n % 2 * 512, n % 2 * 512 + 512)
                eng.wait_ge(fin_ready, n + 1)
                eng.dma_start(out[0, t * P:(t + 1) * P, cols], X[:, t, cols]).then_inc(out_written, 16)
            eng.wait_ge(out_written, 16 * 2 * NT)

        @block.gpsimd
        def _(eng):
            step = steps(eng, pool_step)
            step(eng.memset(UB[:, :], 0.0), u_zero)
            step(eng.memset(IDENT[:, :], 0.0))
            step(eng.memset(ONES[:, :], 1.0), ones_set)
            step(eng.memset(TRI[:, :], 1.0))
            step(eng.memset(MF[:, :], 1.0))
            step(eng.memset(MB[:, :], 1.0))
            step(eng.affine_select(out=IDENT[:, :], in_=IDENT[:, :], compare_op=ALU.not_equal, fill=1.0, base=0,
                                   pattern=[[-1, P]], channel_multiplier=1))
            step(eng.affine_select(out=TRI[:, :], in_=TRI[:, :], compare_op=ALU.is_gt, fill=0.0, base=0,
                                   pattern=[[1, P]], channel_multiplier=-1))
            for h in range(2):
                rows = slice(CH * h, CH * h + CH)
                step(eng.affine_select(out=MF[rows, :], in_=MF[rows, :], compare_op=ALU.is_ge, fill=0.0, base=0,
                                       pattern=[[1, CH]], channel_multiplier=-1))
                step(eng.affine_select(out=MB[rows, :], in_=MB[rows, :], compare_op=ALU.is_gt, fill=0.0, base=0,
                                       pattern=[[-1, CH]], channel_multiplier=1))
            step(eng.iota(IOS[:, :], pattern=[[1, CAP]], base=1, channel_multiplier=0, allow_small_or_imprecise_dtypes=True))
            step(eng.iota(IO32[:, :], pattern=[[1, NE]], base=0, channel_multiplier=0, allow_small_or_imprecise_dtypes=True))
            step(eng.iota(IOT, pattern=[[-P, NT], [1, SEQ]], base=0, channel_multiplier=-1))
            step(eng.iota(SELI[:, 0, :], pattern=[[-1, NE]], base=NE, channel_multiplier=1), iotas)
            eng.wait_ge(b1_in, 48)
            eng.wait_ge(qka_turned, 6)
            step(eng.memset(B1P, 0.0))
            for r in range(3):
                rows = slice(32 * r, 32 * r + 32)
                for part in range(r + 1):
                    step(eng.tensor_copy(B1P[rows, :], B1S[rows, :]), b1p_ready if part == r else pool_step)
                    if part < r:
                        step(eng.tensor_tensor(B1S[rows, :], B1S[rows, :], B1P[rows, :], ALU.subtract))

        @block.scalar
        def _(eng):
            step = steps(eng, act_step)
            act = eng.activation

            def sum_squares(col, junk, n, ready=None):
                step(act(MX[:, 31:32], ONES[:, 0:1], ACT.Sqrt))
                for t in range(NT):
                    if ready:
                        eng.wait_ge(*ready[t])
                    step(act(junk[:, t * D:(t + 1) * D], X[:, t, :], ACT.Square, accum_out=SS[:, col + t:col + t + 1]), squares)
                eng.wait_ge(inv_ready, n)
                step(act(SS[:, col:col + NT], SS[:, col:col + NT], ACT.Sqrt), rms_ready)

            for i, v in enumerate((norm_mix[0], norm_ffn[0], norm_ple[0], out_norm[0].rearrange("a b -> (a b)"),
                                   fgate_bias[0].rearrange("a b -> (a b)"))):
                eng.dma_start(VEC[8 * i:8 * i + 8, :], v.rearrange("(k p) -> k p", p=P)).then_inc(vec_in, 16)
            eng.wait_ge(ones_set, 1)
            sum_squares(0, JUNK, 1, [(x_in[t], 16) for t in range(NT)])
            with nc.allow_non_contiguous_dma(reason="256 positions"):
                eng.dma_start(POSI[:, :], positions[0].rearrange("(t p) -> p t", p=P)).then_inc(pos_in, 16)
            eng.wait_ge(u_zero, 1)
            for d in range(2):
                eng.dma_start(UB[RANK * d:RANK * d + RANK, 512 * d:512 * d + 512], fgate_up[0, d]).then_inc(u_in, 16)
            eng.dma_start(RW[:, :, :], router_w[0].rearrange("(k p) n -> p k n", p=P)).then_inc(small_in, 16)
            eng.dma_start(RB[:, :], router_b).then_inc(small_in, 16)
            eng.wait_ge(ang_ready, 1)
            step(act(CS[:, :, :], ANG[:, :, :], ACT.Sin), trig)

            def slab_banks(i):
                eng.wait_ge(slab_done, i + 1)
                return 2 * (i % 2)

            b = slab_banks(1)
            step(act(QK_T[:, 0:1024], pair(b), ACT.Copy, scale=float(DK) ** -0.5), slab_act)
            b = slab_banks(2)
            step(act(QK_T[:, 1024:2048], pair(b), ACT.Copy), slab_act)
            eng.wait_ge(z_done, 1)
            for c in range(8):
                ins = act(G_B0[:, c * SEQ:(c + 1) * SEQ], bank(4 + c // 2, SEQ, c % 2 * SEQ), ACT.Identity,
                          bias=COL[:, 32 + c:33 + c])
            step(ins, z_read)
            step(act(G_B1, G_B0, ACT.Abs))
            step(act(G_B1, G_B1, ACT.Exp, scale=-1.0))
            step(act(G_B1, G_B1, ACT.Ln, bias=1.0), lse_part)
            eng.wait_ge(diff, 1)
            step(act(G_E, G_D, ACT.Exp, scale=1 / TAU), expd)
            step(act(G_B0, G_D, ACT.Exp, scale=-1 / TAU), expd)
            eng.wait_ge(expd_used, 1)
            step(act(G_E, G_B1, ACT.Exp, scale=1 / TAU), expd)
            eng.wait_ge(diff, 2)
            step(act(G_B0, G_D, ACT.Exp, scale=1 / TAU), expd)
            gb = G_B1.rearrange("p (f c i) -> p f c i", c=NCH, i=CH)
            decv = DEC[:, :].rearrange("p (f c) -> p f c", c=NCH)
            step(act(decv[:, 0:GH, :], gb[:, 0:GH, :, CH - 1], ACT.Exp, scale=1 / TAU), expd)
            step(act(decv[:, GH:, :], gb[:, GH:, :, 0], ACT.Exp, scale=1 / TAU), expd)
            for i in (5, 6, 7):
                b = slab_banks(i)
                for t in range(NT):
                    ins = act(QKA[:, t, (i - 5) * 512:(i - 4) * 512], bank(b + t), ACT.Copy)
                step(ins, slab_act)
            for n in range(4):
                t, d = n // 2, n % 2
                eng.wait_ge(kst_turned, n + 1)
                if n == 0:
                    eng.wait_ge(expd_used, 2)
                step(act(KSTOK[:, t, d * 512:d * 512 + 512], bank(6 + n % 2), ACT.Copy), kstok_ready)
            for i in (10, 11):
                b = slab_banks(i)
                for t in range(NT):
                    ins = act(R[:, t, (i - 10) * 512:(i - 9) * 512], bank(b + t), ACT.Sigmoid)
                step(ins, sil)
            eng.wait_ge(o_done, 1)
            for t in range(NT):
                for h in range(GH):
                    step(act(YJUNK[:, 0:DV], PS[:, 4 + 2 * t + h // 2, h % 2 * DV:h % 2 * DV + DV], ACT.Square,
                             accum_out=SS[:, 4 + GH * t + h:5 + GH * t + h]), o_sq)
            eng.wait_ge(inv_ready, 2)
            step(act(SS[:, 4:4 + NT * GH], SS[:, 4:4 + NT * GH], ACT.Sqrt), rms_ready)
            b = slab_banks(12)
            step(act(GA[:, 0:4, :].rearrange("p k s -> p (k s)"), pair(b), ACT.Sigmoid), slab_act)
            for n in range(6):
                eng.wait_ge(qka_turned, n + 1)
                step(act(QKAT[:, 2 * n:2 * n + 2, :].rearrange("p c s -> p (c s)"), bank(4 + n % 4), ACT.Copy), qkat_ready)

            def gates_a(i):
                b = slab_banks(i)
                dst = (GA, GA, GB, GB)[i - 12][:, 4 * (i % 2):4 * (i % 2) + 4, :]
                step(act(dst.rearrange("p k s -> p (k s)"), pair(b), ACT.Sigmoid), slab_act)

            def soft(h):
                for t in range(NT):
                    u = NT * h + t
                    eng.wait_ge(att_max, u + 1)
                    if h:
                        eng.wait_ge(att_t, u - 1)
                    step(act(PROB[t], SCO[t], ACT.Exp, scale=HD ** -0.5, bias=MX[:, 8 + u:9 + u],
                             accum_out=MX[:, 16 + u:17 + u]), att_exp)

            def pt_copy(h):
                for t in range(NT):
                    eng.wait_ge(att_t, NT * h + t + 1)
                    if h and t == 0:
                        eng.wait_ge(att_o, h)
                    src = PS[:, 4 + 2 * t:6 + 2 * t, :].rearrange("p b n -> p (b n)")[:, 0:768]
                    step(act(PT[:, :, t * P:(t + 1) * P], src.rearrange("p (c i) -> p c i", i=P), ACT.Copy), pt_ready)

            soft(0)
            gates_a(13)
            pt_copy(0)
            soft(1)
            gates_a(14)
            pt_copy(1)
            soft(2)
            gates_a(15)
            pt_copy(2)
            soft(3)
            pt_copy(3)
            eng.wait_ge(p_turned, 1)
            step(act(PTT.rearrange("p k s -> p (k s)"), bank(0), ACT.Copy), ptt_ready)
            sum_squares(2, YJUNK, 3, [(x_mixed, 2), (x_mixed, 4)])
            for t in range(NT):
                ins = act(H[:, t, :], X[:, t, :], ACT.Copy, scale=SS[:, 2 + t:3 + t])
            step(ins, h_ready)
            eng.wait_ge(logits_max, 1)
            for t in range(NT):
                ins = act(TW[:, t, 0:TOPK], TOP[:, t, 0:TOPK], ACT.Exp, bias=MX[:, t:t + 1], accum_out=MX[:, 2 + t:3 + t])
            step(ins, top_exp)

            def embedding(t):
                eng.wait_ge(pp_done, t + 1)
                act(PP[:, t, :], pair(6), ACT.Copy).then_inc(pp_ready, 1)

            embedding(0)

            def sigmoid(n):
                eng.wait_ge(gate_in, n)
                past(eng, a_ready, n - 1)
                act(SIG, GATE, ACT.Sigmoid, scale=ALPHA).then_inc(sig_ready, 1)

            def a_copy(n):
                eng.wait_ge(at_done, n)
                past(eng, oe_done, n - 1)
                act(AT, bank(5), ACT.Copy).then_inc(at_ready, 1)

            def out_copy(n):
                eng.wait_ge(oe_done, n)
                past(eng, sc_done, 2 * n - 2)
                act(OUTE, bank(4), ACT.Copy).then_inc(oe_ready, 1)

            def moe(q):
                def one(i):
                    n = (q * PAIRS + i) * 2
                    sigmoid(n + 1)
                    if isinstance(n, int):
                        embedding(1)
                    eng.wait_ge(tg_done, q * PAIRS + i + 1)
                    past(eng, sc_done, 2 * n)
                    act(GT.rearrange("p e t s -> p (e t s)"), bank(4), ACT.Copy).then_inc(gt_ready, 1)
                    a_copy(n + 1)
                    out_copy(n + 1)
                    sigmoid(n + 2)
                    a_copy(n + 2)
                    out_copy(n + 2)

                one(0)
                with eng.Fori(1, PAIRS) as i:
                    one(i)

            runtime_pass(eng, moe)
            eng.wait_ge(x_final, 1)
            sum_squares(12, YJUNK, 4)
            for t in range(NT):
                for c in range(2):
                    n = 2 * t + c
                    cols = slice(c * 512, c * 512 + 512)
                    eng.wait_ge(pleg_done, n + 1)
                    step(act(H[:, t, cols], bank(n), ACT.Sigmoid, scale=SS[:, 12 + t:13 + t]), ple_sig)
                    if c:
                        step(act(MX[:, 31:32], ONES[:, 0:1], ACT.Sqrt))
                    eng.wait_ge(x_final, 2 + n)
                    step(act(H[:, t, cols], X[:, t, cols], ACT.Square, accum_out=SS[:, 4 + n:5 + n]), squares)
                eng.wait_ge(inv_ready, 5 + t)
                step(act(SS[:, 14 + t:15 + t], SS[:, 14 + t:15 + t], ACT.Sqrt), rms_ready)

        @block.vector
        def _(eng):
            step = steps(eng, dve_step)
            tt, ts, stt = eng.tensor_tensor, eng.tensor_scalar, eng.scalar_tensor_tensor

            def invert(s, n):
                step(ts(s, s, 1.0 / n, EPS, ALU.mult, ALU.add))
                step(eng.reciprocal(s, s), inv_ready)
                inverted[0] += 1
                eng.wait_ge(rms_ready, inverted[0])

            inverted = [0]

            def normed(col):
                invert(SS[:, col:col + NT], D)
                for t in range(NT):
                    step(ts(H[:, t, :], X[:, t, :], SS[:, col + t:col + t + 1], None, ALU.mult), h_ready)

            def turn_copy(use, dst, col):
                for j in range(4):
                    eng.wait_ge(turned, 4 * use + j + 1)
                    step(tt(dst[:, 2 * j:2 * j + 2, :], bank(4 + j).rearrange("p (c s) -> p c s", c=2),
                            COL[:, col + 2 * j:col + 2 * j + 2].unsqueeze(2).broadcast_to([P, 2, SEQ]), ALU.mult), turn_read)

            for j in range(HALF):
                ins = eng.memset(INVF[:, j:j + 1], float(np.float32(THETA) ** np.float32(-2.0 * j / ROT)))
            step(ins)
            for t in range(NT):
                eng.wait_ge(x_in[t], 16)
            eng.wait_ge(squares, 2)
            normed(0)
            eng.wait_ge(vec_turned, 1)
            step(eng.tensor_copy(COL[:, :], bank(7, 40)), cols_ready)
            turn_copy(0, HT, 0)
            eng.wait_ge(slab_done, 1)
            step(eng.tensor_copy(LOWT[:, :], PS[0:2 * RANK, 0, 0:SEQ]), slab_dve)
            eng.wait_ge(pos_in, 16)
            step(eng.tensor_copy(POSF[:, :], POSI[:, :]))
            for v in range(2):
                step(tt(ANG[:, v, :].rearrange("p (t j) -> p t j", j=HALF), POSF[:, :].unsqueeze(2).broadcast_to([P, NT, HALF]),
                        INVF[:, :].unsqueeze(1).broadcast_to([P, NT, HALF]), ALU.mult))
            two_pi = 2 * math.pi
            c1 = 6.28125
            c2 = float(np.float32((two_pi - c1) * 2 ** 20).astype(np.int32)) / 2 ** 20
            c3 = two_pi - c1 - c2
            for v, turn in ((0, 0.25), (1, 0.0)):
                step(ts(TRN[:, v, :], ANG[:, v, :], 1 / two_pi, turn, ALU.mult, ALU.add))
            step(eng.tensor_copy(TURN_I[:, :, :], TRN[:, :, :]))
            step(eng.tensor_copy(TRN[:, :, :], TURN_I[:, :, :]))
            for c in (c1, c2, c3):
                step(stt(out=ANG[:, :, :], in0=TRN[:, :, :], scalar=-c, in1=ANG[:, :, :], op0=ALU.mult, op1=ALU.add))
            step(ts(ANG[:, 0, :], ANG[:, 0, :], math.pi / 2, None, ALU.add))
            pi_in = float(np.nextafter(np.float32(math.pi), np.float32(0)))
            step(ts(ANG[:, :, :], ANG[:, :, :], pi_in, -pi_in, ALU.min, ALU.max), ang_ready)
            eng.wait_ge(iotas, 1)
            am = AM.rearrange("p t (g j) -> p t g j", g=GROUPS)
            step(tt(IOT2, IOT, IOT, ALU.mult))
            step(ts(am[:, :, 0, :], IOT2, 64.0 * 64.0, None, ALU.is_le))
            for g, dil in ((1, 4), (2, 16)):
                step(ts(IOT2, IOT, dil - 1, None, ALU.bitwise_and))
                step(ts(am[:, :, g, :], IOT2, 0.0, None, ALU.is_equal))
            step(eng.memset(SELT[:, :], 0.0))
            step(ts(SELI[:, 1, :], SELI[:, 0, :], NE - 1, None, ALU.bitwise_and))
            for r in range(3):
                step(ts(SELT[32 * r:32 * r + 32, :], SELI[32 * r:32 * r + 32, 1, :], 0.0, None, ALU.is_equal))
            step(ts(SEL4[:, :], SELI[:, 1, :], 0.0, None, ALU.is_equal))
            eng.wait_ge(lse_part, 1)
            step(eng.memset(RESET, 1.0))
            step(eng.memset(RESET.rearrange("p (c i) -> p c i", i=CH)[:, :, 0], 0.0))
            step(stt(out=G_B0, in0=G_B0, scalar=0.0, in1=G_B1, op0=ALU.min, op1=ALU.subtract))
            half = GH * SEQ
            step(eng.tensor_tensor_scan(G_B1[:, 0:half], RESET, G_B0[:, 0:half], 0.0, ALU.mult, ALU.add))
            step(eng.tensor_tensor_scan(G_B1[:, 2 * half - 1:half - 1:-1], RESET, G_B0[:, 2 * half - 1:half - 1:-1],
                                        0.0, ALU.mult, ALU.add), g_cum)

            def empty_to(i, dst):
                eng.wait_ge(slab_done, i + 1)
                w = SLABS[i][1]
                for t in range(NT):
                    ins = eng.tensor_copy(dst[:, t, :], bank(2 * (i % 2) + t, w))
                step(ins, slab_dve)

            chunks = lambda v, d: v[:, d * half:(d + 1) * half].rearrange("p (c i) -> p c i", i=CH)
            q2 = QK_T[:, 0:half].unsqueeze(1).broadcast_to([P, 2, half])
            k2 = QK_T[:, half:2 * half].unsqueeze(1).broadcast_to([P, 2, half])
            two = lambda v: v.rearrange("p (d f) -> p d f", d=2)

            def difference(refs, sign):
                for d in range(2):
                    b = chunks(G_B1, d)
                    ref = b[:, :, refs[d]:refs[d] + 1].broadcast_to([P, GH * NCH, CH])
                    x0, x1 = (b, ref) if sign > 0 else (ref, b)
                    ins = tt(chunks(G_D, d), x0, x1, ALU.subtract)
                step(ins, diff)

            difference((CH // 2 - 1, CH // 2), 1)
            empty_to(3, V[:, :, 0:512])
            eng.wait_ge(slab_act, 2)
            eng.wait_ge(expd, 1)
            step(tt(two(QT_), two(G_E), q2, ALU.mult), expd_used)
            eng.wait_ge(expd, 2)
            step(tt(two(KT_), two(G_B0), k2, ALU.mult), qt_ready)
            difference((CH - 1, 0), -1)
            empty_to(4, V[:, :, 512:1024])
            eng.wait_ge(expd, 3)
            step(tt(two(QIN), two(G_E), q2, ALU.mult), expd_used)
            eng.wait_ge(expd, 4)
            step(tt(two(KST), two(G_B0), k2, ALU.mult), kst_ready)
            eng.wait_ge(trig, 1)
            eng.wait_ge(slab_act, 5)
            heads = QKA.rearrange("p t (h e) -> p t h e", e=HD)
            for t in range(NT):
                t1, t2 = heads[:, t, :, 0:HALF], heads[:, t, :, HALF:ROT]
                cos, sin = (CS[:, v, t * HALF:(t + 1) * HALF].unsqueeze(1).broadcast_to([P, 2 * AHEADS, HALF]) for v in range(2))
                rb = [b[:, t] for b in ROTB]
                step(tt(rb[0], t1, cos, ALU.mult))
                step(tt(rb[1], t2, sin, ALU.mult))
                step(tt(rb[2], t2, cos, ALU.mult))
                step(tt(rb[3], t1, sin, ALU.mult))
                step(tt(t1, rb[0], rb[1], ALU.subtract))
                step(tt(t2, rb[2], rb[3], ALU.add), rotated)
            empty_to(8, VA[:, :, 0:512])
            eng.wait_ge(scores_done, 1)
            for m, i in ((MF, 4), (MB, 5)):
                step(eng.copy_predicated(ST[:, :].rearrange("p (f i) -> p f i", i=CH),
                                         m[:, :].bitcast(U32).unsqueeze(1).broadcast_to([P, 8, CH]),
                                         bank(i).rearrange("p (f i) -> p f i", i=CH)), st_ready)
            empty_to(9, VA[:, :, 512:768])
            for s in range(NCH - 1):
                for dh in range(DH):
                    d, h = dh // GH, dh % GH
                    eng.wait_ge(kv_done, 4 * s + dh // 2 + 1)
                    kv = bank(4 + dh // 2, DV, dh % 2 * DV)
                    if s == 0:
                        if dh == 0:
                            eng.wait_ge(expd, 6)
                            eng.wait_ge(kstok_ready, 4)
                        step(eng.tensor_copy(STATE[dh], kv), state_ready)
                    else:
                        c = s if d == 0 else NCH - 1 - s
                        step(stt(out=STATE[8 * s + dh], in0=STATE[8 * (s - 1) + dh],
                                 scalar=DEC[:, dh * NCH + c:dh * NCH + c + 1], in1=kv, op0=ALU.mult, op1=ALU.add), state_ready)
            for i in (10, 11):
                eng.wait_ge(sil, i - 9)
                for t in range(NT):
                    r = R[:, t, (i - 10) * 512:(i - 9) * 512]
                    ins = tt(r, r, bank(2 * (i % 2) + t), ALU.mult)
                step(ins, slab_dve)
            eng.wait_ge(o_sq, 2 * GH)
            invert(SS[:, 4:4 + NT * GH], DV)
            for t in range(NT):
                for h in range(GH):
                    r = R[:, t, h * DV:(h + 1) * DV]
                    step(stt(out=r, in0=PS[:, 4 + 2 * t + h // 2, h % 2 * DV:h % 2 * DV + DV],
                             scalar=SS[:, 4 + GH * t + h:5 + GH * t + h], in1=r, op0=ALU.mult, op1=ALU.mult), y_ready)
            turn_copy(1, YT, 24)

            for t in range(NT):
                step(eng.memset(SCO[t], NEG))

            def softmax_in(h):
                for t in range(NT):
                    u = NT * h + t
                    eng.wait_ge(att_s, u + 1)
                    if h:
                        eng.wait_ge(att_exp, u - 1)
                    src = PS[:, 4 + 2 * t:6 + 2 * t, :].rearrange("p b n -> p (b n)")[:, 0:768]
                    step(eng.copy_predicated(SCO[t], AM[:, t, :].bitcast(U32), src), att_masked)
                    step(eng.reduce_max(MX[:, u:u + 1], SCO[t], AX))
                    step(ts(MX[:, 8 + u:9 + u], MX[:, u:u + 1], -HD ** -0.5, None, ALU.mult), att_max)

            def softmax_out(h):
                for t in range(NT):
                    u = NT * h + t
                    eng.wait_ge(att_exp, u + 1)
                    step(eng.reciprocal(MX[:, 24 + u:25 + u], MX[:, 16 + u:17 + u]))
                    step(ts(PROB[t], PROB[t], MX[:, 24 + u:25 + u], None, ALU.mult), att_prob)

            def ya_copy(h):
                eng.wait_ge(att_o, h + 1)
                rows = slice(HD * (h % 2), HD * (h % 2) + HD)
                step(eng.tensor_copy(YAT[rows, h // 2, :], PS[rows, 6, 0:SEQ]), yat_ready)

            def branch_a(j):
                eng.wait_ge(a_done, j + 1)
                g = GA[:, 2 * j:2 * j + 2, :].rearrange("p c s -> p (c s)")
                step(tt(g, g, bank(j), ALU.mult), a_used)

            eng.wait_ge(qkat_ready, 6)
            for h in range(AH):
                softmax_in(h)
                softmax_out(h)
                if h == AH - 1:
                    branch_a(0)
                    branch_a(1)
                ya_copy(h)
            branch_a(2)
            branch_a(3)
            for j in range(4):
                eng.wait_ge(b_done, j + 1)
                ga, gb = (g[:, 2 * j:2 * j + 2, :].rearrange("p c s -> p (c s)") for g in (GA, GB))
                step(tt(gb, gb, bank(j), ALU.mult))
                step(tt(ga, ga, gb, ALU.add), m_ready)
            for n in range(4):
                t, c = n // 2, n % 2
                eng.wait_ge(mix_done, n + 1)
                xv = X[:, t, c * 512:c * 512 + 512]
                step(tt(xv, xv, bank(4 + n), ALU.add), x_mixed)
            turn_copy(2, HT, 8)
            eng.wait_ge(squares, 4)
            invert(SS[:, 2:2 + NT], D)
            eng.wait_ge(part_done, 1)
            step(eng.tensor_copy(LPART, bank(1, SEQ)), part_ready)
            step(eng.tensor_copy(RBB[:, :], bank(2, NE)))
            eng.wait_ge(log_done, 1)
            for t in range(NT):
                step(stt(out=LOG[:, t, :], in0=bank(3, NE, t * NE), scalar=SS[:, 2 + t:3 + t], in1=RBB[:, :], op0=ALU.mult, op1=ALU.add))
            for t in range(NT):
                step(eng.max(TOP[:, t, :], LOG[:, t, :]))
                step(eng.max_index(TOPI[:, t, :], TOP[:, t, :], LOG[:, t, :]))
            step(eng.tensor_copy(TOPF[:, :, :], TOPI[:, :, :]))
            step(ts(MX[:, 0:NT], TOP[:, :, 0], -1.0, None, ALU.mult), logits_max)
            four = [P, NT, TOPK, NE]
            hit = HITS.rearrange("p (t k e) -> p t k e", t=NT, k=TOPK)
            step(tt(hit, IO32[:, :].unsqueeze(1).unsqueeze(1).broadcast_to(four),
                    TOPF[:, :, 0:TOPK].unsqueeze(3).broadcast_to(four), ALU.is_equal))
            step(eng.reduce_sum(SEL[:, :, :], HITS.rearrange("p (t k e) -> p t e k", t=NT, k=TOPK), AX), sel_ready)
            eng.wait_ge(rank_done, 1)
            step(stt(out=RANKS[:, :, :].rearrange("p t e -> p (t e)"), in0=bank(5, NT * NE), scalar=1.0,
                     in1=SEL[:, :, :].rearrange("p t e -> p (t e)"), op0=ALU.add, op1=ALU.mult))

            def weights():
                eng.wait_ge(top_exp, 1)
                step(eng.reciprocal(MX[:, 4:4 + NT], MX[:, 2:2 + NT]))
                step(tt(TW[:, :, 0:TOPK], TW[:, :, 0:TOPK], MX[:, 4:4 + NT].unsqueeze(2).broadcast_to([P, NT, TOPK]), ALU.mult))
                step(tt(hit, hit, TW[:, :, 0:TOPK].unsqueeze(3).broadcast_to(four), ALU.mult))
                step(eng.reduce_sum(GATES[:, :, :], HITS.rearrange("p (t k e) -> p t e k", t=NT, k=TOPK), AX), gates_ready)
                eng.wait_ge(rank_done, 2)
                step(eng.reduce_max(CNT[:, :], bank(4, NE), AX))
                step(eng.tensor_copy(CNTI[:, :], CNT[:, :]), flag_ready)

            def choose(j):
                step1(tt(ONEHOT[:, :, :, :], IOS[:, :].unsqueeze(1).unsqueeze(1).broadcast_to([P, NT, 2, CAP]),
                         RANKS[:, :, bass.ds(2 * j, 2)].unsqueeze(3).broadcast_to([P, NT, 2, CAP]), ALU.is_equal))

            def step1(ins):
                ins.then_inc(onehot, 1)

            def weigh(j, n):
                eng.wait_ge(onehot, n)
                for e in range(2):
                    ins = tt(GD[:, e, :, :].rearrange("p t (u s) -> p t u s", u=2),
                             ONEHOT[:, :, e, :].unsqueeze(2).broadcast_to([P, NT, 2, CAP]),
                             GATES[:, :, bass.ds(2 * j + e, 1)].unsqueeze(3).broadcast_to([P, NT, 2, CAP]), ALU.mult)
                ins.then_inc(gd_ready, 1)

            def selector(j, n):
                past(eng, bias_done, n)
                eng.tensor_copy(SELE[:, :, :], SELT[:, bass.ds(2 * j, 2)].unsqueeze(2).broadcast_to([P, 2, CAP])
                                ).then_inc(sele_ready, 1)

            def gathered(n):
                eng.wait_ge(ga_done, n)
                tt(HTE, pair(2).rearrange("p (k s) -> p k s", k=KC),
                   COL[:, 8:16].unsqueeze(2).broadcast_to([P, KC, 2 * CAP]), ALU.mult).then_inc(ht_ready, 1)

            def swiglu(n):
                hid = pair(0).rearrange("p (f u) -> p f u", u=2)
                eng.wait_ge(hid_done, n)
                eng.tensor_scalar(GATE, hid[:, :, 0], LIMIT, None, ALU.min).then_inc(gate_in, 1)
                ts(UP, hid[:, :, 1], LIMIT, -LIMIT, ALU.min, ALU.max).then_inc(hid_read, 1)
                eng.wait_ge(hid_read, n)
                stt(out=UP, in0=UP, scalar=1.0, in1=GATE, op0=ALU.add, op1=ALU.mult).then_inc(glu_part, 1)
                eng.wait_ge(glu_part, n)
                eng.wait_ge(sig_ready, n)
                past(eng, at_done, n - 1)
                tt(A, UP, SIG, ALU.mult).then_inc(a_ready, 1)

            def add_x(n, t, b=6):
                eng.wait_ge(sc_done, 2 * n - 1 + t)
                tt(X[:, t, :], X[:, t, :], pair(b), ALU.add).then_inc(x_added, 1)

            def moe(q):
                first = q * PAIRS
                if not isinstance(q, int):
                    ts(IOS[:, :], IOS[:, :], float(CAP), None, ALU.add).then_inc(ios_moved, 1)
                    eng.wait_ge(ios_moved, q)
                    eng.wait_ge(tg_done, first)
                    eng.wait_ge(gd_ready, first)
                choose(0)
                selector(0, 2 * first)
                if isinstance(q, int):
                    weights()
                gathered(first + 1)
                if isinstance(q, int):
                    eng.wait_ge(gatt_done, 1)
                    step(eng.tensor_copy(GATT[:, :], PS[0:NE, 4, 0:SEQ]), gatt_ready)
                weigh(0, first + 1)

                def one(i, begins, last):
                    m = first + i
                    n = 2 * m
                    if not last:
                        eng.wait_ge(ga_done, m + 1)
                        eng.wait_ge(gd_ready, m + 1)
                        choose(i + 1)
                    if not begins:
                        add_x(n, 0)
                        add_x(n, 1)
                    swiglu(n + 1)
                    if not last:
                        eng.wait_ge(tg_done, m + 1)
                        weigh(i + 1, m + 2)
                    if not last:
                        add_x(n + 1, 0)
                        selector(i + 1, n + 2)
                    swiglu(n + 2)
                    if not last:
                        add_x(n + 1, 1)
                        gathered(m + 2)
                    else:
                        add_x(n + 1, 0)
                        add_x(n + 1, 1, 2)
                        add_x(n + 2, 0)
                        add_x(n + 2, 1, 2)

                one(0, True, False)
                with eng.Fori(1, PAIRS - 1) as i:
                    one(i, False, False)
                one(PAIRS - 1, False, True)

            runtime_pass(eng, moe)
            step(eng.memset(CNT[:, :], 0.0), x_final)
            turn_copy(3, HT, 16)
            eng.wait_ge(squares, 6)
            invert(SS[:, 12:12 + NT], D)
            eng.wait_ge(nf_in, 16)
            for t in range(NT):
                for c in range(2):
                    n = 2 * t + c
                    cols = slice(c * 512, c * 512 + 512)
                    eng.wait_ge(ple_sig, n + 1)
                    step(tt(H[:, t, cols], H[:, t, cols], PP[:, t, cols], ALU.mult))
                    step(tt(X[:, t, cols], X[:, t, cols], H[:, t, cols], ALU.add), x_final)
                eng.wait_ge(squares, 8 + 2 * t)
                step(tt(SS[:, 14 + t:15 + t], SS[:, 4 + 2 * t:5 + 2 * t], SS[:, 5 + 2 * t:6 + 2 * t], ALU.add))
                invert(SS[:, 14 + t:15 + t], D)
                for c in range(2):
                    cols = slice(c * 512, c * 512 + 512)
                    stt(out=X[:, t, cols], in0=X[:, t, cols], scalar=SS[:, 14 + t:15 + t], in1=NF[:, cols],
                        op0=ALU.mult, op1=ALU.mult).then_inc(fin_ready, 1)

        @block.tensor
        def _(eng):
            mm = eng.matmul
            eng.wait_ge(iotas, 1)
            eng.wait_ge(vec_in, 80)
            eng.transpose(bank(7, 40), VEC[:, :], IDENT[0:40, 0:40]).then_inc(vec_turned, 1)

            def turn(use, src):
                for j in range(4):
                    for c in range(2):
                        for t in range(NT):
                            f = (2 * j + c) * P
                            ins = eng.transpose(bank(4 + j, P, c * SEQ + t * P), src[:, t, f:f + P], IDENT[:, :])
                    ins.then_inc(turned, 1)

            eng.wait_ge(h_ready, 2)
            eng.wait_ge(cols_ready, 1)
            turn(0, H)

            def slab(i, part=None):
                c0, w, by_feature = SLABS[i]
                if not part:
                    eng.wait_ge(slab_in[i % 2], 16 * (i // 2 + 1))
                    if i >= 2:
                        mine, n = emptied(i - 2)
                        eng.wait_ge(slab_dve if mine else slab_act, n)
                wv = SLAB[i % 2]
                if by_feature:
                    for c in range(-(-w // P)) if part is None else [part]:
                        m = min(P, w - c * P)
                        for k in range(KC):
                            ins = mm(PS[0:m, 2 * (i % 2) + c // 2, c % 2 * SEQ:c % 2 * SEQ + SEQ], wv[:, k, c * P:c * P + m],
                                     HT[:, k, :], start=k == 0, stop=k == KC - 1)
                else:
                    for t in range(NT):
                        for k in range(KC):
                            ins = mm(bank(2 * (i % 2) + t, w), HT[:, k, t * P:(t + 1) * P], wv[:, k, 0:w],
                                     start=k == 0, stop=k == KC - 1)
                if part in (None, 3):
                    ins.then_inc(slab_done, 1)

            eng.wait_ge(turn_read, 4)
            for i in range(3):
                slab(i)
            eng.wait_ge(u_in, 32)
            eng.wait_ge(slab_dve, 1)
            for c in range(8):
                ins = mm(bank(4 + c // 2, SEQ, c % 2 * SEQ), UB[:, c * P:(c + 1) * P], LOWT[:, :], start=True, stop=True)
            ins.then_inc(z_done, 1)
            for i in range(3, 9):
                slab(i)
            eng.wait_ge(qt_ready, 1)
            eng.wait_ge(z_read, 1)
            for d in range(2):
                for h in range(GH):
                    for c in range(NCH):
                        f = (d * GH + h) * SEQ + c * CH
                        rows = slice(c % 2 * CH, c % 2 * CH + CH)
                        ins = mm(PS[rows, 4 + d, h * P + c // 2 * CH:h * P + c // 2 * CH + CH], KT_[:, f:f + CH],
                                 QT_[:, f:f + CH], start=True, stop=True)
            ins.then_inc(scores_done, 1)
            eng.wait_ge(kst_ready, 1)
            for n in range(4):
                t, d = n // 2, n % 2
                if n >= 2:
                    eng.wait_ge(kstok_ready, n - 1)
                for h in range(GH):
                    f = (d * GH + h) * SEQ + t * P
                    ins = eng.transpose(bank(6 + n % 2, DK, h * DK), KST[:, f:f + P], IDENT[:, :])
                ins.then_inc(kst_turned, 1)
            slab(9)
            eng.wait_ge(slab_dve, 3)
            eng.wait_ge(st_ready, 2)
            eng.wait_ge(kstok_ready, 4)
            for s in range(NCH - 1):
                for dh in range(DH):
                    d, h = dh // GH, dh % GH
                    c = s if d == 0 else NCH - 1 - s
                    rows = slice(c % 2 * CH, c % 2 * CH + CH)
                    if s:
                        eng.wait_ge(state_ready, 8 * (s - 1) + 2 * (dh // 2) + 2)
                    ins = mm(bank(4 + dh // 2, DV, dh % 2 * DV), KSTOK[rows, c // 2, dh * DK:(dh + 1) * DK],
                             V[rows, c // 2, h * DV:(h + 1) * DV], start=True, stop=True)
                    if dh % 2:
                        ins.then_inc(kv_done, 1)
            slab(10)
            eng.wait_ge(state_ready, 8 * (NCH - 1))
            for c in range(NCH):
                t, rows = c // 2, slice(c % 2 * CH, c % 2 * CH + CH)
                for h in range(GH):
                    o = PS[rows, 4 + 2 * t + h // 2, h % 2 * DV:h % 2 * DV + DV]
                    parts = [(ST[rows, h * P + t * CH:h * P + t * CH + CH], V[rows, t, h * DV:(h + 1) * DV])]
                    if c > 0:
                        parts.append((QIN[:, h * SEQ + c * CH:h * SEQ + c * CH + CH], STATE[8 * (c - 1) + h]))
                    if c < NCH - 1:
                        f = (GH + h) * SEQ + c * CH
                        parts.append((QIN[:, f:f + CH], STATE[8 * (NCH - 2 - c) + GH + h]))
                    for n, (l, r) in enumerate(parts):
                        ins = mm(o, l, r, start=n == 0, stop=n == len(parts) - 1)
            ins.then_inc(o_done, 1)
            slab(11)
            slab(12)
            eng.wait_ge(y_ready, 8)
            turn(1, R)
            slab(13, 0)
            eng.wait_ge(rotated, 2)
            eng.wait_ge(turn_read, 8)
            for n in range(6):
                if n >= 4:
                    eng.wait_ge(qkat_ready, n - 3)
                for c in range(2):
                    for t in range(NT):
                        f = (2 * n + c) * P
                        ins = eng.transpose(bank(4 + n % 4, P, c * SEQ + t * P), QKA[:, t, f:f + P], IDENT[:, :])
                ins.then_inc(qka_turned, 1)

            def scores(h):
                rows = slice(HD * (h % 2), HD * (h % 2) + HD)
                if h == 0:
                    eng.wait_ge(qkat_ready, 6)
                else:
                    eng.wait_ge(pt_ready, NT * h)
                    eng.wait_ge(yat_ready, h)
                for t in range(NT):
                    for g in range(GROUPS):
                        c = (g * AH + h) // 2
                        ins = mm(PS[:, 4 + 2 * t + g // 2, g % 2 * SEQ:g % 2 * SEQ + SEQ], QKAT[rows, c, t * P:(t + 1) * P],
                                 QKAT[rows, 6 + c, :], start=True, stop=True)
                    ins.then_inc(att_s, 1)

            def probs(h):
                for t in range(NT):
                    eng.wait_ge(att_prob, NT * h + t + 1)
                    for c in range(6):
                        ins = eng.transpose(PS[:, 4 + 2 * t + c // 4, c % 4 * P:c % 4 * P + P], PROB[t][:, c * P:(c + 1) * P],
                                            IDENT[:, :])
                    ins.then_inc(att_t, 1)

            def head_out(h):
                eng.wait_ge(pt_ready, NT * h + NT)
                if h == 0:
                    eng.wait_ge(slab_dve, 5)
                rows = slice(HD * (h % 2), HD * (h % 2) + HD)
                for c in range(6):
                    head, jt = c // 2 * AH + h, c % 2
                    ins = mm(PS[rows, 6, 0:SEQ], VA[:, jt, head * HD:(head + 1) * HD], PT[:, c, :], start=c == 0, stop=c == 5)
                ins.then_inc(att_o, 1)

            def branch(j, wv, src, nk, done, half=None):
                for c in (2 * j, 2 * j + 1) if half is None else [2 * j + half]:
                    for k in range(nk):
                        ins = mm(bank(j, SEQ, c % 2 * SEQ), wv[:, k, c * P:(c + 1) * P], src[:, k, :], start=k == 0, stop=k == nk - 1)
                if half != 0:
                    ins.then_inc(done, 1)

            def branch_a(j, half):
                if j % 2 == 0 and half == 0:
                    eng.wait_ge(slab_act, emptied(14 + j // 2)[1])
                if j == 0 and half == 0:
                    eng.wait_ge(wa_in, 16)
                branch(j, W_A, YT, KC, a_done, half)

            slab(13, 1)
            scores(0)
            slab(13, 2)
            slab(13, 3)
            probs(0)
            slab(14, 0)
            head_out(0)
            slab(14, 1)
            scores(1)
            slab(14, 2)
            slab(14, 3)
            probs(1)
            slab(15, 0)
            head_out(1)
            slab(15, 1)
            scores(2)
            slab(15, 2)
            slab(15, 3)
            probs(2)
            branch_a(0, 0)
            head_out(2)
            branch_a(0, 1)
            scores(3)
            branch_a(1, 0)
            branch_a(1, 1)
            probs(3)
            branch_a(2, 0)
            head_out(3)
            branch_a(2, 1)
            branch_a(3, 0)
            branch_a(3, 1)
            eng.wait_ge(yat_ready, AH)
            eng.wait_ge(wb_in, 16)
            for j in range(4):
                eng.wait_ge(a_used, j + 1)
                branch(j, W_B, YAT, 2, b_done)
            eng.wait_ge(p_in, 32)
            eng.wait_ge(m_ready, 1)
            for c in range(2):
                for t in range(NT):
                    ins = eng.transpose(bank(0, P, c * SEQ + t * P), PTOK[:, t, c * P:(c + 1) * P], IDENT[:, :])
            ins.then_inc(p_turned, 1)
            eng.wait_ge(wout_in, 16)
            for n in range(4):
                t, c = n // 2, n % 2
                for k in range(KC):
                    if n == 0 and k % 2 == 0:
                        eng.wait_ge(m_ready, k // 2 + 1)
                    ins = mm(bank(4 + n), GA[:, k, t * P:(t + 1) * P], W_OUT[:, k, c * 512:c * 512 + 512], start=k == 0, stop=k == KC - 1)
                ins.then_inc(mix_done, 1)
            eng.wait_ge(small_in, 32)
            mm(bank(2, NE), ONES[0:1, :], RB[:, :], start=True, stop=True)
            eng.wait_ge(x_mixed, 4)
            turn(2, X)
            for i in range(2):
                for g in range(4):
                    k = 2 * g + i
                    eng.wait_ge(turn_read, 9 + g)
                    ins = mm(PS[NE * g:NE * g + NE, 1, 0:SEQ], RW[:, k, :], HT[:, k, :], start=i == 0, stop=i == 1)
            ins.then_inc(part_done, 1)
            eng.wait_ge(part_ready, 1)
            for t in range(NT):
                ins = mm(bank(3, NE, t * NE), LPART[:, t * P:(t + 1) * P], SEL4[:, :], start=True, stop=True)
            ins.then_inc(log_done, 1)

            def embed(t, c):
                for k in range(2):
                    ins = mm(bank(6 + c), PTT[:, k, t * P:(t + 1) * P], W_P[:, k, c * 512:c * 512 + 512], start=k == 0, stop=k == 1)
                if c:
                    ins.then_inc(pp_done, 1)

            eng.wait_ge(ptt_ready, 1)
            embed(0, 0)
            eng.wait_ge(sel_ready, 1)
            mm(bank(5, NT * NE), TRI[:, :], SEL[:, :, :].rearrange("p t e -> p (t e)"), start=True, stop=False)
            mm(bank(5, NE, NE), ONES[:, :], SEL[:, 0, :], start=False, stop=True).then_inc(rank_done, 1)
            for t in range(NT):
                ins = mm(bank(4, NE), ONES[:, :], SEL[:, t, :], start=t == 0, stop=t == NT - 1)
            ins.then_inc(rank_done, 1)

            def gather(n, chunks):
                if chunks[0] == 0:
                    eng.wait_ge(onehot, n)
                    past(eng, ht_ready, n - 1)
                for k in chunks:
                    for t in range(NT):
                        ins = mm(PS[:, 2 + k // 4, k % 4 * P:k % 4 * P + P], H[:, t, k * P:(k + 1) * P],
                                 ONEHOT[:, t, :, :].rearrange("p e s -> p (e s)"), start=t == 0, stop=t == NT - 1)
                if chunks[-1] == KC - 1:
                    ins.then_inc(ga_done, 1)

            def bias(n, e, m):
                eng.wait_ge(sele_ready, m)
                past(eng, hid_read, n - 1)
                for c in range(4):
                    h = CAP * (c // 2)
                    ins = mm(PS[h:h + CAP, c % 2, :], SELE[:, e, :], B1P[:, c * 512:c * 512 + 512], start=True, stop=False)
                ins.then_inc(bias_done, 1)

            def hidden(n, e, m, between={}):
                for k in range(KC):
                    if k in between:
                        scatter(*between[k])
                    eng.wait_ge(land1[e][k], (m if k < TWICE else n) * 16)
                    for c in (0, 2, 1, 3):
                        h = CAP * (c // 2)
                        ins = mm(PS[h:h + CAP, c % 2, :], HTE[:, k, e * CAP:(e + 1) * CAP], W1[e][k][:, c * 512:c * 512 + 512],
                                 start=False, stop=k == KC - 1)
                    if k < KC - 1:
                        ins.then_inc(w_used, 1)
                ins.then_inc(hid_done, 1)

            def down(n, e, m):
                eng.wait_ge(at_ready, n)
                for f in range(KC):
                    if f % 2 == 0:
                        eng.wait_ge(land2[e][f // 2], m * 16)
                    for h in range(2):
                        ins = mm(PS[CAP * h:CAP * h + CAP, 4, :], AT[:, f % 4 * P + f // 4 * CAP:f % 4 * P + f // 4 * CAP + CAP],
                                 W2[e][f // 2][:, f % 2 * D + h * 512:f % 2 * D + h * 512 + 512], start=f == 0, stop=f == KC - 1)
                    if f % 2 and f < KC - 1:
                        ins.then_inc(w_used, 1)
                ins.then_inc(oe_done, 1)

            def turn_a(n):
                eng.wait_ge(a_ready, n)
                past(eng, at_ready, n - 1)
                for c in range(4):
                    ins = eng.transpose(bank(5, P, c * P), A[:, c * P:(c + 1) * P], IDENT[:, :])
                ins.then_inc(at_done, 1)

            def scatter(n, e, t, b=6):
                eng.wait_ge(oe_ready, n)
                if b == 6:
                    past(eng, x_added, 2 * n - 2 + t)
                first = isinstance(n, int) and n == 1
                for h in range(2):
                    if first:
                        if h == 0:
                            eng.wait_ge(b2_in, 16)
                            eng.wait_ge(pp_ready, 2)
                        mm(bank(6 + h), GATT[:, t * P:(t + 1) * P], UB[:, h * 512:h * 512 + 512], start=True, stop=False)
                for h in range(2):
                    ins = mm(bank(b + h), GT[CAP * h:CAP * h + CAP, e, t, :], OUTE[CAP * h:CAP * h + CAP, :], start=not first, stop=True)
                ins.then_inc(sc_done, 1)

            def moe(q):
                first = q * PAIRS
                if isinstance(q, int):
                    eng.wait_ge(h_ready, 3)
                gather(first + 1, range(KC))
                if isinstance(q, int):
                    embed(0, 1)
                    eng.wait_ge(gates_ready, 1)
                    eng.wait_ge(flag_ready, 1)
                    for t in range(NT):
                        ins = eng.transpose(PS[0:NE, 4, t * P:(t + 1) * P], GATES[:, t, :], IDENT[:, :])
                    ins.then_inc(gatt_done, 1)
                    eng.wait_ge(b1p_ready, 3)

                bias(2 * first + 1, 0, first + 1)

                def one(i, begins, last):
                    m = first + i
                    n = 2 * m
                    eng.wait_ge(ht_ready, m + 1)
                    hidden(n + 1, 0, m + 1, {} if begins else {2: (n, 1, 0), 5: (n, 1, 1)})
                    if isinstance(m, int) and begins:
                        eng.wait_ge(pp_ready, 1)
                        embed(1, 0)
                        embed(1, 1)
                    eng.wait_ge(gd_ready, m + 1)
                    past(eng, oe_ready, n)
                    if isinstance(m, int):
                        eng.wait_ge(gatt_ready, 1)
                    for e in range(2):
                        for t in range(NT):
                            ins = eng.transpose(bank(4, P, (2 * e + t) * P), GD[:, e, t, :], IDENT[:, :])
                    ins.then_inc(tg_done, 1)
                    if not last:
                        gather(m + 2, range(KC - 2))
                    turn_a(n + 1)
                    bias(n + 2, 1, m + 1)
                    eng.wait_ge(gt_ready, m + 1)
                    down(n + 1, 0, m + 1)
                    hidden(n + 2, 1, m + 1, {} if last else {4: (n + 1, 0, 0)})
                    if not last:
                        gather(m + 2, range(KC - 2, KC))
                        scatter(n + 1, 0, 1)
                    else:
                        scatter(n + 1, 0, 0)
                        scatter(n + 1, 0, 1, 2)
                    turn_a(n + 2)
                    if not last:
                        bias(n + 3, 0, m + 2)
                    eng.wait_ge(oe_ready, n + 1)
                    down(n + 2, 1, m + 1)
                    if last:
                        scatter(n + 2, 1, 0)
                        eng.wait_ge(x_added, 2 * n + 2)
                        scatter(n + 2, 1, 1, 2)

                one(0, True, False)
                with eng.Fori(1, PAIRS - 1) as i:
                    one(i, False, False)
                one(PAIRS - 1, False, True)
                if not isinstance(q, int):
                    eng.wait_ge(wg_in[0], q * 16 + 16)
                    eng.wait_ge(wg_in[1], q * 16 + 16)
                    eng.nop()

            runtime_pass(eng, moe)
            eng.wait_ge(x_final, 1)
            turn(3, X)
            for n in range(4):
                t, c = n // 2, n % 2
                for k in range(KC):
                    if n == 0 and k % 2 == 0:
                        eng.wait_ge(turn_read, 13 + k // 2)
                    if n == 0 and k % 4 == 0:
                        eng.wait_ge(wg_in[k // 4], 16)
                    ins = mm(bank(n), HT[:, k, t * P:(t + 1) * P], W_G[:, k, c * 512:c * 512 + 512], start=k == 0, stop=k == KC - 1)
                ins.then_inc(pleg_done, 1)


_INS = ["x", "p", "positions", "norm_mix", "w_in", "gla_fgate_up", "gla_fgate_bias", "gla_out_norm", "w_branch_gla",
        "w_branch_attn", "w_out", "norm_ffn", "router_w", "router_b", "expert_w1", "expert_b1", "expert_w2", "expert_b2",
        "norm_ple", "ple_gate_w", "ple_proj", "norm_final"]


def kernel(**inputs):
    import numpy as _np
    import concourse.bacc as _bacc
    from concourse import mybir as _mybir
    from concourse.bass_utils import run_bass_kernel_spmd as _run

    nc = _bacc.Bacc("TRN2", target_bir_lowering=False, num_devices=1)
    arrays, args = {}, []
    for name in _INS:
        a = _np.ascontiguousarray(inputs[name])
        arrays[f"in_{name}"] = a
        args.append(nc.dram_tensor(f"in_{name}", a.shape, _mybir.dt.from_np(a.dtype), kind="ExternalInput").ap())
    args.append(nc.dram_tensor("out_0", (1, SEQ, D), _mybir.dt.float32, kind="ExternalOutput").ap())
    build(nc, *args)
    r = _run(nc, [arrays], core_ids=[0])
    return r.results[0]["out_0"]
```
